# Optimizing a Trainium2 kernel written in Bass

```python
import jax, jax.numpy as jnp
from jax import lax
import numpy as np

D_MODEL = 1024
BATCH = 1
SEQ = 512
DEPTH = 1

D_FF = 2816
POOL_WIDTH = D_MODEL // 2
POOL_WINDOWS = (2, 4, 8, 16)
N_POOL_GROUPS = len(POOL_WINDOWS)
POOL_GROUP = POOL_WIDTH // N_POOL_GROUPS
HEAD_DIM = 64
N_HEADS = D_MODEL // HEAD_DIM
N_KV_HEADS = N_HEADS // 8
GQA_GROUP = N_HEADS // N_KV_HEADS
WINDOW = 128
BLOCK = 128
ATTN_WIDTH = N_HEADS * HEAD_DIM
KV_WIDTH = N_KV_HEADS * HEAD_DIM
N_BRANCHES = 2
IN_WIDTH = POOL_WIDTH + ATTN_WIDTH + 2 * KV_WIDTH + N_BRANCHES * D_MODEL
RMS_EPS = 1e-6

kernel_name = "hybrid_pool_swa_sink_macaron_layer"

def rmsnorm(x, g):
    xf = x.astype(jnp.float32)
    y = xf * lax.rsqrt(jnp.mean(xf * xf, axis=-1, keepdims=True) + RMS_EPS)
    return (y * g.astype(jnp.float32)).astype(x.dtype)

def swiglu(x, w_gate, w_up, w_down):
    return (jax.nn.silu(x @ w_gate) * (x @ w_up)) @ w_down

def causal_pool_mixer(xp, pool_w, pool_scale):
    B, S, P = xp.shape
    xf = xp.astype(jnp.float32)
    csum = jnp.concatenate([jnp.zeros((B, 1, P), jnp.float32), jnp.cumsum(xf, axis=1)], axis=1)
    t = jnp.arange(S)
    pooled = []
    for gi, w in enumerate(POOL_WINDOWS):
        cg = csum[..., gi * POOL_GROUP:(gi + 1) * POOL_GROUP]
        start = jnp.maximum(t + 1 - w, 0)
        window_sum = cg[:, 1:, :] - cg[:, start, :]
        count = jnp.minimum(t + 1, w).astype(jnp.float32)
        pooled.append(window_sum / count[None, :, None])
    pooled = (jnp.concatenate(pooled, axis=-1) - xf).astype(xp.dtype)
    pooled = pooled.reshape(B, S, N_POOL_GROUPS, POOL_GROUP)
    mixed = jnp.einsum('bsgc,gcd->bsgd', pooled, pool_w).reshape(B, S, P)
    return mixed * pool_scale

def sliding_window_sink_attention(q, k, v, q_norm, k_norm, sinks):
    B, S = q.shape[0], q.shape[1]
    nb = S // BLOCK
    q = rmsnorm(q, q_norm)
    k = rmsnorm(k, k_norm)
    qb = q.reshape(B, nb, BLOCK, N_KV_HEADS, GQA_GROUP, HEAD_DIM)
    kb = k.reshape(B, nb, BLOCK, N_KV_HEADS, HEAD_DIM)
    vb = v.reshape(B, nb, BLOCK, N_KV_HEADS, HEAD_DIM)
    pad = ((0, 0), (1, 0), (0, 0), (0, 0), (0, 0))
    kk = jnp.concatenate([jnp.pad(kb, pad)[:, :-1], kb], axis=2)
    vv = jnp.concatenate([jnp.pad(vb, pad)[:, :-1], vb], axis=2)
    scores = jnp.einsum('bnqhgd,bnkhd->bnhgqk', qb, kk).astype(jnp.float32) * (HEAD_DIM ** -0.5)
    qi = jnp.arange(BLOCK)[:, None]
    kj = jnp.arange(2 * BLOCK)[None, :] - BLOCK
    rel = qi - kj
    band = (rel >= 0) & (rel < WINDOW)
    in_seq = (jnp.arange(nb)[:, None, None] > 0) | (kj[None] >= 0)
    mask = band[None] & in_seq
    scores = jnp.where(mask[None, :, None, None], scores, jnp.finfo(jnp.float32).min)
    sink = jnp.broadcast_to(sinks.astype(jnp.float32).reshape(1, 1, N_KV_HEADS, GQA_GROUP, 1, 1),
                            scores.shape[:-1] + (1,))
    probs = jax.nn.softmax(jnp.concatenate([scores, sink], axis=-1), axis=-1)[..., :-1]
    out = jnp.einsum('bnhgqk,bnkhd->bnqhgd', probs.astype(vv.dtype), vv)
    return out.reshape(B, S, ATTN_WIDTH)

def setup_inputs(seed: int = 0) -> dict:
    key = jax.random.key(seed)
    ks = jax.random.split(key, 24)
    f32 = jnp.float32

    def nrm(k, shape, fan_in):
        return jax.random.normal(k, shape, f32) * (fan_in ** -0.5)

    def gain(k, shape):
        return jnp.ones(shape, f32) + 0.02 * jax.random.normal(k, shape, f32)

    return {
        "x": jax.random.normal(ks[0], (BATCH, SEQ, D_MODEL), f32),
        "ffn1_norm": gain(ks[1], (D_MODEL,)),
        "ffn1_w_gate": nrm(ks[2], (D_MODEL, D_FF), D_MODEL),
        "ffn1_w_up": nrm(ks[3], (D_MODEL, D_FF), D_MODEL),
        "ffn1_w_down": nrm(ks[4], (D_FF, D_MODEL), D_FF),
        "mix_norm": gain(ks[5], (D_MODEL,)),
        "w_in": nrm(ks[6], (D_MODEL, IN_WIDTH), D_MODEL),
        "pool_w": nrm(ks[7], (N_POOL_GROUPS, POOL_GROUP, POOL_GROUP), POOL_GROUP),
        "pool_scale": gain(ks[8], (POOL_WIDTH,)),
        "w_pool_out": nrm(ks[9], (POOL_WIDTH, D_MODEL), POOL_WIDTH),
        "q_norm": gain(ks[10], (HEAD_DIM,)),
        "k_norm": gain(ks[11], (HEAD_DIM,)),
        "sinks": 0.5 * jax.random.normal(ks[12], (N_HEADS,), f32),
        "w_attn_out": nrm(ks[13], (ATTN_WIDTH, D_MODEL), ATTN_WIDTH),
        "gate_bias": 0.01 * jax.random.normal(ks[14], (N_BRANCHES * D_MODEL,), f32),
        "w_out": nrm(ks[15], (D_MODEL, D_MODEL), D_MODEL),
        "ffn2_norm": gain(ks[16], (D_MODEL,)),
        "ffn2_w_gate": nrm(ks[17], (D_MODEL, D_FF), D_MODEL),
        "ffn2_w_up": nrm(ks[18], (D_MODEL, D_FF), D_MODEL),
        "ffn2_w_down": nrm(ks[19], (D_FF, D_MODEL), D_FF),
    }

def reference(x, ffn1_norm, ffn1_w_gate, ffn1_w_up, ffn1_w_down, mix_norm, w_in, pool_w,
              pool_scale, w_pool_out, q_norm, k_norm, sinks, w_attn_out, gate_bias, w_out,
              ffn2_norm, ffn2_w_gate, ffn2_w_up, ffn2_w_down):
    B, S, _ = x.shape
    h = x
    for _layer in range(DEPTH):
        h = h + 0.5 * swiglu(rmsnorm(h, ffn1_norm), ffn1_w_gate, ffn1_w_up, ffn1_w_down)
        u = rmsnorm(h, mix_norm)
        proj = u @ w_in
        o = 0
        xp = proj[..., o:o + POOL_WIDTH]; o += POOL_WIDTH
        q = proj[..., o:o + ATTN_WIDTH].reshape(B, S, N_HEADS, HEAD_DIM); o += ATTN_WIDTH
        k = proj[..., o:o + KV_WIDTH].reshape(B, S, N_KV_HEADS, HEAD_DIM); o += KV_WIDTH
        v = proj[..., o:o + KV_WIDTH].reshape(B, S, N_KV_HEADS, HEAD_DIM); o += KV_WIDTH
        gates = jax.nn.sigmoid(proj[..., o:o + N_BRANCHES * D_MODEL] + gate_bias)
        gate_pool = gates[..., :D_MODEL]
        gate_attn = gates[..., D_MODEL:]
        branch_pool = causal_pool_mixer(xp, pool_w, pool_scale) @ w_pool_out
        branch_attn = sliding_window_sink_attention(q, k, v, q_norm, k_norm, sinks) @ w_attn_out
        merged = gate_pool * branch_pool + gate_attn * branch_attn
        h = h + merged @ w_out
        h = h + 0.5 * swiglu(rmsnorm(h, ffn2_norm), ffn2_w_gate, ffn2_w_up, ffn2_w_down)
    return h


_drawn_inputs = setup_inputs


def setup_inputs(seed=0):
    import zlib

    import numpy as np

    out = dict(_drawn_inputs(seed))
    spreads = {}
    factors = {'ffn1_norm': 6.111,
     'mix_norm': 5.659,
     'pool_scale': 20.523,
     'q_norm': 45.022,
     'k_norm': 45.226,
     'sinks': 200.0,
     'gate_bias': 33.041,
     'ffn2_norm': 24.849}
    for name, (base, spread) in spreads.items():
        noise = np.random.default_rng([zlib.crc32(name.encode()), seed]).standard_normal(out[name].shape)
        drawn = base * np.exp(spread * noise) if base else spread * noise
        out[name] = __import__('jax').numpy.asarray(drawn.astype(out[name].dtype))
    for name, factor in factors.items():
        out[name] = (out[name] * factor).astype(out[name].dtype)
    return out
```

```python
from contextlib import ExitStack

import numpy as np

import concourse.bass as bass
from concourse import mybir

F32 = mybir.dt.float32
F32R = mybir.dt.float32r
ALU = mybir.AluOpType
ACT = mybir.ActivationFunctionType

P = 128
TOK = 512
D = 1024
DT = D // P
FF = 2816
FT = FF // P
POOL_WINDOWS = (2, 4, 8, 16)
PG = len(POOL_WINDOWS)
PAD = max(POOL_WINDOWS)
HD = 64
KV = 2
QT = 8
BLK = 128
NB = TOK // BLK
EPS = 1e-6
MASKED = -1e30

SLOTS = 4
TILES = 8
UNIT = TILES * P
HALF = DT // 2
DOWN = FT * HALF // TILES

U_GU1 = 0
U_DN1 = U_GU1 + 2 * FT
U_POOL = U_DN1 + 2 * DOWN
U_K = U_POOL + PG
U_V = U_K + 1
U_Q = U_V + 1
U_PO = U_Q + QT
U_GATE = U_PO + PG
U_AO = U_GATE + 2 * DT
U_WO = U_AO + DT
U_GU2 = U_WO + DT
U_DN2 = U_GU2 + 2 * FT
UNITS = U_DN2 + 2 * DOWN

C_ONES, C_ID, C_HEADS, C_MASK, C_INV = 0, 128, 256, 384, 640
CONSTS = C_INV + PG * PAD
P_N1, P_MIX, P_N2, P_PSC, P_QN, P_KN, P_BIAS, P_SINK = 0, 8, 16, 24, 28, 29, 30, 46
PARAMS = 62


def layer_kernel(nc, x_in, consts_in, params_in, poolw_in, weights_in, out):
    ctx = ExitStack()
    with ctx:
        def sb(name, shape, dt=F32, at=ctx):
            return at.enter_context(nc.sbuf_tensor(name, shape, dt))

        def sem(name):
            return ctx.enter_context(nc.semaphore(name))

        h = sb("h", [P, DT, TOK])
        raw = sb("w_raw", [P, SLOTS, UNIT])
        high = sb("w_high", [P, SLOTS, UNIT], F32R)
        low = sb("w_low", [P, SLOTS, UNIT], F32R)
        consts = sb("consts", [P, CONSTS])
        params = sb("params", [P, PARAMS])
        half_bias = sb("half_bias", [P, 2 * DT])
        rinv = sb("rinv", [P, TOK])
        sq = sb("squares", [P, 2, TOK])
        gt = sq
        acc = sb("sum_of_squares", [P, TOK])
        ones = consts[:, C_ONES:C_ONES + P]
        ident = consts[:, C_ID:C_ID + P]
        same_head = consts[:, C_HEADS:C_HEADS + P]
        head_cols = consts[:, C_HEADS:C_HEADS + P:HD]

        with ExitStack() as u_scope:
            uh = sb("u_high", [P, DT, TOK], F32R, u_scope)
            ul = sb("u_low", [P, DT, TOK], F32R, u_scope)
            with ExitStack() as s:
                ffn1 = dict(
                    hid_h=sb("hid1_high", [P, FT, TOK], F32R, s), hid_l=sb("hid1_low", [P, FT, TOK], F32R, s),
                    gate=sb("gate1", [P, 2, TOK], F32, s), tanh=sb("tanh1", [P, 2, TOK], F32, s),
                    up=sb("up1", [P, 2, TOK], F32, s))
            with ExitStack() as s:
                pb = sb("pool_branch", [P, DT, TOK], F32, s)
                with ExitStack() as t:
                    kraw = sb("k_raw", [P, TOK], F32, t)
                    vraw = sb("v_raw", [P, TOK], F32, t)
                    qsq = sb("q_squares", [P, 2, TOK], F32, t)
                    pw_raw = sb("poolw_raw", [P, PG * P], F32, t)
                    pw_h = sb("poolw_high", [P, PG * P], F32R, t)
                    pw_l = sb("poolw_low", [P, PG * P], F32R, t)
                th_attn = sb("tanh_gate_attn", [P, DT, TOK], F32, s)
                kn = sb("k_normed", [P, BLK + TOK], F32, s)
                vtok = sb("v_tokens", [P, 1 + NB, P], F32, s)
                rq = sb("rq", [P, NB * QT * KV], F32, s)
                qtmp = sb("rq_tmp", [P, 3, NB * QT * KV], F32, s)
                with ExitStack() as t:
                    q = sb("q", [P, QT, TOK], F32, t)
                with ExitStack() as t:
                    oh = sb("attn_high", [P, QT, TOK], F32R, t)
                    with ExitStack() as v:
                        pl_h = sb("pooled_high", [P, PG, TOK], F32R, v)
                        pl_l = sb("pooled_low", [P, PG, TOK], F32R, v)
                    ol = sb("attn_low", [P, QT, TOK], F32R, t)
                    with ExitStack() as v:
                        mix_h = sb("mixed_high", [P, PG, TOK], F32R, v)
                        mix_l = sb("mixed_low", [P, PG, TOK], F32R, v)
                        xp = sb("pool_in", [P, PAD + TOK], F32, v)
                        win = sb("window_sums", [P, 2, PAD + TOK], F32, v)
                        pooled = sb("pooled", [P, TOK], F32, v)
                    with ExitStack() as v:
                        qs_h = sb("q_block_high", [P, QT, BLK], F32R, v)
                        qs_l = sb("q_block_low", [P, QT, BLK], F32R, v)
                        ks_h = sb("k_block_high", [P, 2 * BLK], F32R, v)
                        ks_l = sb("k_block_low", [P, 2 * BLK], F32R, v)
                        vs_h = sb("v_block_high", [P, 2, P], F32R, v)
                        vs_l = sb("v_block_low", [P, 2, P], F32R, v)
                        prob = sb("probs", [P, 2, 4, 2 * BLK], F32, v)
                        pt_h = sb("probsT_high", [P, 2, 4 * BLK], F32R, v)
                        pt_l = sb("probsT_low", [P, 2, 4 * BLK], F32R, v)
                        mask = sb("mask_now", [P, 2 * BLK], F32, v)
                        smax = sb("raw_max", [P, 2, 4], F32, v)
                        msink = sb("sink_minus_max", [P, 2, 4], F32, v)
                        smx = sb("score_max", [P, 2, 4], F32, v)
                        nmax = sb("neg_max", [P, 2, 4], F32, v)
                        rows = sb("row_sums", [P, 2, 4], F32, v)
                        esink = sb("exp_sink", [P, 2, 4], F32, v)
                        den = sb("denominator", [P, 2, 4], F32, v)
                        rden = sb("inv_denominator", [P, 2, 4], F32, v)
                        spare = sb("spare", [P, 1], F32, v)
                        rqn = sb("rq_now", [P, QT * KV], F32, v)
        with ExitStack() as s:
            mg_h = sb("merged_high", [P, DT, TOK], F32R, s)
            mg_l = sb("merged_low", [P, DT, TOK], F32R, s)
        with ExitStack() as s:
            ffn2 = dict(
                hid_h=sb("hid2_high", [P, FT, TOK], F32R, s), hid_l=sb("hid2_low", [P, FT, TOK], F32R, s),
                gate=sb("gate2", [P, 2, TOK], F32, s), tanh=sb("tanh2", [P, 2, TOK], F32, s),
                up=sb("up2", [P, 2, TOK], F32, s))
            uh2 = sb("u2_high", [P, DT, TOK], F32R, s)
            ul2 = sb("u2_low", [P, DT, TOK], F32R, s)
        psum = ctx.enter_context(nc.psum_tensor("psum", [P, 8, TOK], F32))

        raw_landed = [sem(f"raw_landed{s}") for s in range(SLOTS)]
        high_done = sem("high_done")
        low_done = sem("low_done")
        unit_used = sem("unit_used")
        small_landed = sem("small_landed")
        poolw_landed = sem("poolw_landed")
        x_landed = [sem(f"x_landed{i}") for i in range(DT // 2)]
        init_done = sem("init_done")
        pw_high = sem("pw_high")
        pw_low = sem("pw_low")
        h_ready = [None] + [sem(f"h_ready{n}") for n in (1, 2)]
        u_high = [sem(f"u_high_done{n}") for n in range(3)]
        u_low = [sem(f"u_low_done{n}") for n in range(3)]
        squared = [sem(f"squared{n}") for n in range(3)]
        summed = [sem(f"summed{n}") for n in range(3)]
        ss_ready = sem("ss_ready")
        var_ready = sem("var_ready")
        root_ready = sem("root_ready")
        link = sem("vector_link")
        for n, f in enumerate((ffn1, ffn2)):
            for name in ("gate_scaled", "gate_tanh", "gate_silu", "up_scaled", "hidden", "hidden_high",
                         "hidden_low", "down_tile"):
                f[name] = sem(f"ffn{n + 1}_{name}")
        pool_scaled = sem("pool_scaled")
        pooled_ready = sem("pooled_ready")
        pooled_high = sem("pooled_high_done")
        pooled_low = sem("pooled_low_done")
        mixed_done = sem("mixed_done")
        mixed_high = sem("mixed_high_done")
        mixed_low = sem("mixed_low_done")
        k_scaled = sem("k_scaled")
        k_squared = sem("k_squared")
        k_summed = sem("k_summed")
        k_var = sem("k_var")
        k_root = sem("k_root")
        k_ready = sem("k_ready")
        v_scaled = sem("v_scaled")
        v_turned = sem("v_turned")
        v_ready = sem("v_ready")
        q_ready = sem("q_ready")
        q_squared = sem("q_squared")
        q_summed = sem("q_summed")
        q_var = sem("q_var")
        q_root = sem("q_root")
        rq_ready = sem("rq_ready")
        pb_ready = sem("pb_ready")
        q_block_high = sem("q_block_high_done")
        q_block_low = sem("q_block_low_done")
        k_block_high = sem("k_block_high_done")
        k_block_low = sem("k_block_low_done")
        v_block_high = sem("v_block_high_done")
        v_block_low = sem("v_block_low_done")
        rq_now_ready = sem("rq_now_ready")
        scored = sem("scored")
        mask_set = sem("mask_set")
        masked = sem("masked")
        max_a = sem("max_scaled")
        max_b = sem("max_with_sink")
        max_done = sem("max_done")
        exp_done = sem("exp_done")
        den_done = sem("den_done")
        rden_done = sem("rden_done")
        probs_ready = sem("probs_ready")
        turned = sem("probs_turned")
        pt_high = sem("pt_high_done")
        pt_low = sem("pt_low_done")
        weighed = sem("weighed")
        attn_high = sem("attn_high_done")
        attn_low = sem("attn_low_done")
        gate_scaled = sem("gate_scaled")
        gate_tanh = sem("gate_tanh")
        pool_gated = sem("pool_gated")
        attn_gated = sem("attn_gated")
        merged = sem("merged")
        merged_high = sem("merged_high_done")
        merged_low = sem("merged_low_done")
        final_ready = sem("final_ready")
        stored = sem("stored")

        gains = (params[:, P_N1:P_N1 + DT], params[:, P_MIX:P_MIX + DT], params[:, P_N2:P_N2 + DT])
        u_of = ((uh, ul), (uh, ul), (uh2, ul2))

        def at(t, k, n=1):
            return t[:, bass.ds(k, n)]

        block = ctx.enter_context(nc.Block())

        @block.sync
        def _(sp):
            sp.dma_start(params[:, :], params_in).then_inc(small_landed, 16)

            def load(u, s):
                sp.dma_start(raw[:, s, :], weights_in[bass.ds(u, 1), :, :].rearrange("a p n -> p (a n)")
                             ).then_inc(raw_landed[s], 16)

            load(0, 0)
            load(1, 1)
            sp.dma_start(consts[:, :], consts_in).then_inc(small_landed, 16)
            load(2, 2)
            load(3, 3)
            with sp.Fori(1, UNITS // SLOTS) as i:
                for s in range(SLOTS):
                    sp.wait_ge(low_done, SLOTS * i + s - SLOTS + 1)
                    load(SLOTS * i + s, s)
            for u in range(UNITS // SLOTS * SLOTS, UNITS):
                sp.wait_ge(low_done, u - SLOTS + 1)
                load(u, u % SLOTS)
            for c in range(DT):
                sp.wait_ge(final_ready, c + 1)
                sp.dma_start(out[:, c, :], h[:, c, :]).then_inc(stored, 16)
            sp.wait_ge(stored, 16 * DT)

        @block.tensor
        def _(pe):
            def passes(bank, s, tile, xh, xl, start, stop):
                wh = high[:, s, tile * P:(tile + 1) * P]
                wl = low[:, s, tile * P:(tile + 1) * P]
                o = psum[:, bank, :]
                pe.matmul(o, wh, xh, start=start, stop=False)
                pe.matmul(o, wh, xl, start=False, stop=False)
                return pe.matmul(o, wl, xh, start=False, stop=stop)

            def project(u, s, bank, xh, xl, x_ready=None, tiles=range(TILES)):
                if tiles[0] == 0:
                    pe.wait_ge(low_done, u + 1)
                for c in tiles:
                    if x_ready is not None:
                        pe.wait_ge(x_ready, c + 1)
                    mm = passes(bank, s, c, xh[:, c, :], xl[:, c, :], c == 0, c == TILES - 1)
                if tiles[-1] == TILES - 1:
                    mm.then_inc(unit_used, 1)

            def sum_of_squares(n):
                pe.wait_ge(summed[n], DT + 1)
                pe.matmul(psum[:, 0, :], ones, acc[:, :], start=True, stop=True).then_inc(ss_ready, 1)

            def gate_up(base, f, k, F, xh, xl, x_ready=None, first=False):
                if not first:
                    pe.wait_ge(F["gate_scaled"], f - 1)
                project(base + 2 * f, 2 * k, 4 + 2 * k, xh, xl, x_ready)
                if not first:
                    pe.wait_ge(F["up_scaled"], f - 1)
                project(base + 2 * f + 1, 2 * k + 1, 5 + 2 * k, xh, xl)

            def ffn_up(n, base, F, xh, xl):
                gate_up(base, 0, 0, F, xh, xl, u_low[n], first=True)
                sum_of_squares(n)
                gate_up(base, 1, 1, F, xh, xl, first=True)
                with pe.Fori(1, FT // 2) as i:
                    for k in range(2):
                        gate_up(base, 2 * i + k, k, F, xh, xl)

            def down_unit(u, s, c2, half, F, start=False, stop=False):
                pe.wait_ge(low_done, u + 1)
                for m in range(HALF):
                    for kk in range(2):
                        xh = F["hid_h"][:, bass.ds(2 * c2 + kk, 1), :].rearrange("p a t -> p (a t)")
                        xl = F["hid_l"][:, bass.ds(2 * c2 + kk, 1), :].rearrange("p a t -> p (a t)")
                        mm = passes(HALF * half + m, s, 2 * m + kk, xh, xl,
                                    start and kk == 0, stop and kk == 1)
                    if stop and m < HALF - 1:
                        mm.then_inc(F["down_tile"], 1)
                mm.then_inc(unit_used, 1)

            def ffn_down(base, F):
                for half in range(2):
                    b = base + half * DOWN
                    pe.wait_ge(F["hidden_low"], FT if half else FT - 2)
                    down_unit(b, b % SLOTS, 0, half, F, start=True)
                    with pe.Fori(0, 2) as i:
                        for j in range(SLOTS):
                            down_unit(b + 1 + SLOTS * i + j, (b + 1 + j) % SLOTS, 1 + SLOTS * i + j, half, F)
                    down_unit(b + DOWN - 2, (b + DOWN - 2) % SLOTS, DOWN - 2, half, F)
                    pe.wait_ge(F["hidden_low"], FT)
                    down_unit(b + DOWN - 1, (b + DOWN - 1) % SLOTS, DOWN - 1, half, F, stop=True)

            pe.wait_ge(small_landed, 32)
            ffn_up(0, U_GU1, ffn1, uh, ul)
            ffn_down(U_DN1, ffn1)

            def proj_bank(u):
                return 4 + u % SLOTS

            def proj(u, x_ready=None):
                project(u, u % SLOTS, proj_bank(u), uh, ul, x_ready)

            def pool_mix(g):
                pe.wait_ge(pooled_low, g + 1)
                if g == 0:
                    pe.wait_ge(pw_low, 1)
                if g >= 2:
                    pe.wait_ge(mixed_low, g - 1)
                o, w = psum[:, g % 2, :], slice(g * P, (g + 1) * P)
                pe.matmul(o, pw_h[:, w], pl_h[:, g, :], start=True, stop=False)
                pe.matmul(o, pw_h[:, w], pl_l[:, g, :], start=False, stop=False)
                pe.matmul(o, pw_l[:, w], pl_h[:, g, :], start=False, stop=True).then_inc(mixed_done, 1)

            def q_sums(c):
                pe.wait_ge(q_squared, c + 1)
                for b in range(NB):
                    col = b * QT * KV + c * KV
                    mm = pe.matmul(psum[:, 2, col:col + KV], qsq[:, c % 2, b * BLK:(b + 1) * BLK], head_cols,
                                   start=True, stop=True, skip_group_check=True)
                mm.then_inc(q_summed, 1)

            pe.wait_ge(h_ready[1], DT)
            proj(U_POOL, u_low[1])
            proj(U_POOL + 1)
            sum_of_squares(1)
            proj(U_POOL + 2)
            proj(U_POOL + 3)
            pe.wait_ge(pool_scaled, 1)
            proj(U_K)
            pe.wait_ge(pool_scaled, 2)
            proj(U_V)
            pe.wait_ge(pool_scaled, 3)
            proj(U_Q)
            pe.wait_ge(pool_scaled, 4)
            proj(U_Q + 1)
            q_sums(0)
            pool_mix(0)
            pool_mix(1)
            pe.wait_ge(k_scaled, 1)
            proj(U_Q + 2)
            q_sums(1)
            pool_mix(2)
            pool_mix(3)
            pe.wait_ge(k_squared, 1)
            pe.matmul(psum[:, 3, :], same_head, sq[:, 0, :], start=True, stop=True).then_inc(k_summed, 1)
            pe.wait_ge(v_scaled, 1)
            proj(U_Q + 3)
            q_sums(2)
            pe.wait_ge(k_var, 1)
            for b in range(NB):
                mm = pe.transpose(psum[:, 3, b * P:(b + 1) * P], vraw[:, b * BLK:(b + 1) * BLK], ident)
            mm.then_inc(v_turned, 1)
            for c in range(4, QT):
                pe.wait_ge(q_ready, c - 3)
                proj(U_Q + c)
                q_sums(c - 1)
            pe.wait_ge(mixed_low, PG)
            for i in range(PG):
                u = U_PO + i
                pe.wait_ge(low_done, u + 1)
                if i < 2:
                    pe.wait_ge(q_ready, 6 + 2 * i)
                else:
                    pe.wait_ge(pb_ready, 2 * i - 2)
                for m in range(2):
                    for c in range(PG):
                        mm = passes(4 + 2 * (i % 2) + m, u % SLOTS, m * PG + c, mix_h[:, c, :], mix_l[:, c, :],
                                    c == 0, c == PG - 1)
                mm.then_inc(unit_used, 1)
                if i == 0:
                    q_sums(QT - 1)

            def scores(nb, j):
                pe.wait_ge(masked, 16 * nb + 4 * j + 1)
                if j == 0:
                    pe.wait_ge(q_block_low, nb + 1)
                    pe.wait_ge(k_block_low, nb + 1)
                for hh in range(2):
                    for kv in range(KV):
                        r = slice(kv * HD, (kv + 1) * HD)
                        o = psum[:, 4 + kv, hh * 2 * BLK:(hh + 1) * 2 * BLK]
                        pe.matmul(o, qs_h[r, 2 * j + hh, :], ks_h[r, :], start=True, stop=False)
                        pe.matmul(o, qs_h[r, 2 * j + hh, :], ks_l[r, :], start=False, stop=False)
                        mm = pe.matmul(o, qs_l[r, 2 * j + hh, :], ks_h[r, :], start=False, stop=True)
                mm.then_inc(scored, 1)

            def gate(nb, j, tiles=range(TILES)):
                project(U_GATE + SLOTS * nb + j, j, (1, 2, 3, 2)[j], uh, ul, tiles=tiles)

            def turn(nb, j):
                pe.wait_ge(probs_ready, 4 * nb + j + 1)
                for k in range(2):
                    for a in range(4):
                        hh, kv = a // KV, a % KV
                        col = (kv * 2 + hh) * BLK
                        mm = pe.transpose(psum[:, 6 + k, col:col + BLK], prob[:, j % 2, a, k * BLK:(k + 1) * BLK], ident)
                mm.then_inc(turned, 1)

            def weigh(nb, j):
                pe.wait_ge(pt_low, 8 * nb + 2 * j + 2)
                pe.wait_ge(attn_low, 8 * nb + 2 * j + 1)
                if j == 0:
                    pe.wait_ge(v_block_low, nb + 1)
                o = psum[:, 0, :]
                for k in range(2):
                    pe.matmul(o, vs_h[:, k, :], pt_h[:, k, :], start=(k == 0), stop=False)
                    pe.matmul(o, vs_h[:, k, :], pt_l[:, k, :], start=False, stop=False)
                    mm = pe.matmul(o, vs_l[:, k, :], pt_h[:, k, :], start=False, stop=(k == 1))
                mm.then_inc(weighed, 1)

            def attention_block(nb):
                scores(nb, 0)
                gate(nb, 0)
                scores(nb, 1)
                gate(nb, 1)
                turn(nb, 0)
                scores(nb, 2)
                weigh(nb, 0)
                gate(nb, 2)
                turn(nb, 1)
                scores(nb, 3)
                weigh(nb, 1)
                gate(nb, 3, range(0, TILES // 2))
                turn(nb, 2)
                gate(nb, 3, range(TILES // 2, TILES))
                weigh(nb, 2)
                turn(nb, 3)
                weigh(nb, 3)

            pe.wait_ge(pb_ready, DT)
            with pe.Fori(0, NB - 1) as nb:
                attention_block(nb)
            attention_block(NB - 1)

            pe.wait_ge(attn_low, 8 * NB + 1)
            for j in range(SLOTS):
                project(U_AO + j, j, 4 + j, oh, ol)
            for j in range(SLOTS):
                pe.wait_ge(attn_gated, j + 1)
                project(U_AO + SLOTS + j, j, 4 + j, oh, ol)

            for j in range(SLOTS):
                project(U_WO + j, j, j, mg_h, mg_l, merged_low if j == 0 else None)
            for j in range(SLOTS):
                pe.wait_ge(h_ready[2], j + 1)
                project(U_WO + SLOTS + j, j, j, mg_h, mg_l)

            ffn_up(2, U_GU2, ffn2, uh2, ul2)
            ffn_down(U_DN2, ffn2)

        @block.scalar
        def _(act):
            for i in range(DT // 2):
                act.dma_start(h[:, 2 * i:2 * i + 2, :], x_in[:, 2 * i:2 * i + 2, :]).then_inc(x_landed[i], 16)

            def refill(u, s, i=0, first=False):
                if not first:
                    act.wait_ge(unit_used, u - SLOTS + 1)
                act.wait_ge(raw_landed[s], 16 * i)
                act.activation(high[:, s, :], raw[:, s, :], ACT.Copy).then_inc(high_done, 1)

            def next_unit(u0, i=0):
                refill(u0 + SLOTS + SLOTS * i, u0 % SLOTS, u0 // SLOTS + 2 + i)

            def scale_high(n, c):
                if n:
                    act.wait_ge(h_ready[n], c + 1)
                else:
                    act.wait_ge(x_landed[c // 2], 16)
                act.activation(u_of[n][0][:, bass.ds(c, 1), :], h[:, bass.ds(c, 1), :], ACT.Identity,
                               scale=at(gains[n], c)).then_inc(u_high[n], 1)

            def square(n, c, k):
                act.wait_ge(summed[n], c - 2 + 2 if k >= 2 else 1)
                act.activation(sq[:, k % 2, :], h[:, bass.ds(c, 1), :].rearrange("p a t -> p (a t)"),
                               ACT.Square).then_inc(squared[n], 1)

            def root(n):
                act.wait_ge(var_ready, n + 1)
                act.activation(sq[:, 1, :], sq[:, 0, :], ACT.Sqrt).then_inc(root_ready, 1)

            def ffn_up(base, F):
                with act.Fori(0, FT // 2) as i:
                    for k in range(2):
                        f = 2 * i + k
                        act.wait_ge(F["gate_scaled"], f + 1)
                        act.activation(F["tanh"][:, k, :], F["gate"][:, k, :], ACT.Tanh, scale=0.5
                                       ).then_inc(F["gate_tanh"], 1)
                        next_unit(base + 2 * k, i)
                        next_unit(base + 2 * k + 1, i)
                        act.wait_ge(F["hidden"], f + 1)
                        act.activation(F["hid_h"][:, bass.ds(f, 1), :], F["up"][:, k:k + 1, :], ACT.Copy
                                       ).then_inc(F["hidden_high"], 1)

            def down_half(b, n, half):
                with act.Fori(0, 2) as i:
                    for j in range(SLOTS):
                        next_unit(b + j, i)
                for u in (b + 8, b + 9):
                    if u + SLOTS < UNITS:
                        next_unit(u)
                if n:
                    for j in range(HALF):
                        scale_high(n, HALF * half + j)
                if b + 10 + SLOTS < UNITS:
                    next_unit(b + 10)
                if n:
                    for j in range(HALF):
                        c = HALF * half + j
                        square(n, c, c)

            act.wait_ge(small_landed, 32)
            scale_high(0, 0)
            refill(0, 0, 1, first=True)
            for c in range(1, DT):
                scale_high(0, c)
            refill(1, 1, 1, first=True)
            for c in range(DT):
                square(0, c, c)
                if c == 3:
                    refill(2, 2, 1, first=True)
            refill(3, 3, 1, first=True)
            root(0)
            ffn_up(U_GU1, ffn1)
            down_half(U_DN1, 1, 0)
            down_half(U_DN1 + DOWN, 1, 1)

            def pooled_part(g):
                act.wait_ge(pooled_ready, g + 1)
                act.activation(pl_h[:, g, :], pooled[:, :], ACT.Copy).then_inc(pooled_high, 1)

            def mixed_part(g):
                act.wait_ge(mixed_done, g + 1)
                act.activation(mix_h[:, g, :], psum[:, g % 2, :], ACT.Identity,
                               scale=params[:, P_PSC + g:P_PSC + g + 1]).then_inc(mixed_high, 1)

            def q_square(c):
                act.wait_ge(q_ready, c + 1)
                if c >= 2:
                    act.wait_ge(q_summed, c - 1)
                act.activation(qsq[:, c % 2, :], q[:, c, :], ACT.Square).then_inc(q_squared, 1)

            act.wait_ge(h_ready[1], DT)
            act.dma_start(pw_raw[:, :], poolw_in).then_inc(poolw_landed, 16)
            root(1)
            next_unit(U_POOL)
            act.wait_ge(poolw_landed, 16)
            act.activation(pw_h[:, :], pw_raw[:, :], ACT.Copy).then_inc(pw_high, 1)
            pooled_part(0)
            next_unit(U_POOL + 1)
            pooled_part(1)
            next_unit(U_POOL + 2)
            pooled_part(2)
            next_unit(U_POOL + 3)
            next_unit(U_K)
            pooled_part(3)
            next_unit(U_V)
            act.wait_ge(k_scaled, 1)
            act.activation(sq[:, 0, :], kraw[:, :], ACT.Square).then_inc(k_squared, 1)
            q_square(0)
            next_unit(U_Q)
            mixed_part(0)
            mixed_part(1)
            q_square(1)
            next_unit(U_Q + 1)
            mixed_part(2)
            mixed_part(3)
            q_square(2)
            next_unit(U_Q + 2)
            act.wait_ge(k_var, 1)
            act.activation(sq[:, 0, :], sq[:, 1, :], ACT.Sqrt).then_inc(k_root, 1)
            for c in range(3, QT):
                q_square(c)
                next_unit(U_Q + c)
            for i in range(PG):
                next_unit(U_PO + i)
                for m in range(2):
                    act.activation(pb[:, 2 * i + m, :], psum[:, 4 + 2 * (i % 2) + m, :], ACT.Copy
                                   ).then_inc(pb_ready, 1)
                if i == 1:
                    act.wait_ge(q_var, 1)
                    act.activation(qtmp[:, 1, :], qtmp[:, 0, :], ACT.Sqrt).then_inc(q_root, 1)

            def stage_qk(nb):
                act.wait_ge(masked, 16 * nb + 1)
                act.activation(qs_h[:, :, :], q[:, :, bass.ds(nb * BLK, BLK)], ACT.Identity,
                               scale=params[:, P_QN:P_QN + 1]).then_inc(q_block_high, 1)
                act.activation(ks_h[:, :], kn[:, bass.ds(nb * BLK, 2 * BLK)], ACT.Copy).then_inc(k_block_high, 1)

            def stage_v(nb):
                act.wait_ge(attn_low, 8 * nb + 1)
                act.activation(vs_h[:, :, :], vtok[:, bass.ds(nb, 2), :], ACT.Copy).then_inc(v_block_high, 1)

            def exps(nb, j):
                act.wait_ge(max_done, 8 * nb + 2 * j + 2)
                for a in range(4):
                    act.activation(prob[:, j % 2, a, :], prob[:, j % 2, a, :], ACT.Exp,
                                   bias=nmax[:, j % 2, a:a + 1], scale=rqn[:, 4 * j + a:4 * j + a + 1],
                                   accum_out=rows[:, j % 2, a:a + 1]).then_inc(exp_done, 1)
                act.activation(esink[:, j % 2, :], msink[:, j % 2, :], ACT.Exp).then_inc(exp_done, 1)

            def gate(nb, j):
                act.wait_ge(gate_scaled, 4 * nb + j + 1)
                to = gt[:, j:j + 1, :] if j < 2 else th_attn[:, bass.ds(2 * nb + j - 2, 1), :]
                act.activation(to, gt[:, j % 2:j % 2 + 1, :], ACT.Tanh, scale=0.5,
                               bias=half_bias[:, bass.ds(4 * nb + j, 1)]).then_inc(gate_tanh, 1)

            def turned_part(nb, j):
                act.wait_ge(turned, 4 * nb + j + 1)
                for k in range(2):
                    act.activation(pt_h[:, k, :], psum[:, 6 + k, :], ACT.Copy).then_inc(pt_high, 1)

            def attn_part(nb, j):
                act.wait_ge(weighed, 4 * nb + j + 1)
                for kv in range(KV):
                    r = slice(kv * HD, (kv + 1) * HD)
                    act.activation(oh[r, 2 * j:2 * j + 2, bass.ds(nb * BLK, BLK)],
                                   psum[r, 0, kv * 2 * BLK:(kv + 1) * 2 * BLK].rearrange("p (a t) -> p a t", a=2),
                                   ACT.Copy).then_inc(attn_high, 1)

            def attention_block(nb, last):
                exps(nb, 0)
                next_unit(U_GATE, nb)
                gate(nb, 0)
                exps(nb, 1)
                next_unit(U_GATE + 1, nb)
                gate(nb, 1)
                turned_part(nb, 0)
                exps(nb, 2)
                attn_part(nb, 0)
                next_unit(U_GATE + 2, nb)
                gate(nb, 2)
                turned_part(nb, 1)
                exps(nb, 3)
                attn_part(nb, 1)
                turned_part(nb, 2)
                next_unit(U_GATE + 3, nb)
                gate(nb, 3)
                if not last:
                    stage_qk(nb + 1)
                attn_part(nb, 2)
                turned_part(nb, 3)
                attn_part(nb, 3)
                if not last:
                    stage_v(nb + 1)

            act.wait_ge(q_ready, QT)
            act.wait_ge(k_ready, 2)
            act.wait_ge(v_ready, 2)
            stage_qk(0)
            stage_v(0)
            with act.Fori(0, NB - 1) as nb:
                attention_block(nb, False)
            attention_block(NB - 1, True)

            def merge_part(i, j):
                m = SLOTS * i + j
                next_unit(U_AO + j, i)
                act.wait_ge(merged, m + 1)
                act.activation(mg_h[:, bass.ds(m, 1), :], gt[:, j % 2:j % 2 + 1, :], ACT.Copy).then_inc(merged_high, 1)

            with act.Fori(0, 2) as i:
                for j in range(SLOTS):
                    merge_part(i, j)

            for half in range(2):
                for j in range(SLOTS):
                    c = HALF * half + j
                    next_unit(U_WO + c)
                    scale_high(2, c)
                    square(2, c, c)
            root(2)
            ffn_up(U_GU2, ffn2)
            down_half(U_DN2, 0, 0)
            b = U_DN2 + DOWN
            with act.Fori(0, 1) as i:
                for j in range(SLOTS):
                    next_unit(b + j, i)
            for u in range(b + SLOTS, UNITS - SLOTS):
                next_unit(u)

        @block.gpsimd
        def _(pool):
            def low_part(u, s):
                pool.wait_ge(high_done, u + 1)
                pool.tensor_tensor(low[:, s, :], raw[:, s, :], high[:, s, :], ALU.subtract).then_inc(low_done, 1)

            for s in range(SLOTS):
                low_part(s, s)
            with pool.Fori(1, (U_GATE + SLOTS) // SLOTS) as i:
                for s in range(SLOTS):
                    low_part(SLOTS * i + s, s)

            def stage_k(nb):
                pool.wait_ge(k_block_high, nb + 1)
                pool.tensor_tensor(ks_l[:, :], kn[:, bass.ds(nb * BLK, 2 * BLK)], ks_h[:, :],
                                   ALU.subtract).then_inc(k_block_low, 1)

            def stage_v(nb):
                pool.wait_ge(v_block_high, nb + 1)
                pool.tensor_tensor(vs_l[:, :, :], vtok[:, bass.ds(nb, 2), :], vs_h[:, :, :],
                                   ALU.subtract).then_inc(v_block_low, 1)

            def normalize(nb, j):
                pool.wait_ge(rden_done, 4 * nb + j + 1)
                p = prob[:, j % 2, :, :]
                pool.tensor_tensor(p, p, rden[:, j % 2, :].unsqueeze(2).to_broadcast([P, 4, 2 * BLK]),
                                   ALU.mult).then_inc(probs_ready, 1)

            def attention_block(nb, last):
                for j in range(SLOTS):
                    if j == 3:
                        normalize(nb, j)
                    low_part(U_GATE + SLOTS + SLOTS * nb + j, j)
                    if j < 3:
                        normalize(nb, j)
                if not last:
                    stage_k(nb + 1)
                    stage_v(nb + 1)

            stage_k(0)
            stage_v(0)
            with pool.Fori(0, NB - 1) as nb:
                attention_block(nb, False)
            attention_block(NB - 1, True)
            with pool.Fori(U_AO // SLOTS + 1, UNITS // SLOTS) as i:
                for s in range(SLOTS):
                    low_part(SLOTS * i + s, s)
            for u in range(UNITS // SLOTS * SLOTS, UNITS):
                low_part(u, u % SLOTS)

        @block.vector
        def _(dve):
            steps = [0]

            def then(ins):
                steps[0] += 1
                ins.then_inc(link, 1)
                dve.wait_ge(link, steps[0])

            def tile(t, c):
                return t[:, bass.ds(c, 1), :].rearrange("p a t -> p (a t)")

            def clear_sum(n):
                dve.memset(acc[:, :], 0.0).then_inc(summed[n], 1)

            def scale_low(n, c):
                dve.wait_ge(u_high[n], c + 1)
                hi, lo = u_of[n]
                dve.scalar_tensor_tensor(out=tile(lo, c), in0=tile(h, c), scalar=at(gains[n], c), in1=tile(hi, c),
                                         op0=ALU.mult, op1=ALU.subtract).then_inc(u_low[n], 1)

            def add_square(n, c, k):
                dve.wait_ge(squared[n], c + 1)
                dve.wait_ge(summed[n], c + 1)
                dve.tensor_tensor(acc[:, :], acc[:, :], sq[:, k % 2, :], ALU.add).then_inc(summed[n], 1)

            def residual(n, c, bank, scale, done):
                dve.scalar_tensor_tensor(out=tile(h, c), in0=psum[:, bank, :], scalar=scale, in1=tile(h, c),
                                         op0=ALU.mult, op1=ALU.add).then_inc(done, 1)

            def newton(y, v, t):
                then(dve.tensor_tensor(t, y, y, ALU.mult))
                then(dve.tensor_tensor(t, t, v, ALU.mult))
                then(dve.tensor_scalar(t, t, -0.5, 1.5, ALU.mult, ALU.add))

            def norm_factor(n):
                dve.wait_ge(ss_ready, n + 1)
                dve.tensor_scalar(sq[:, 0, :], psum[:, 0, :], 1.0 / D, EPS, ALU.mult, ALU.add).then_inc(var_ready, 1)
                dve.wait_ge(root_ready, n + 1)
                then(dve.reciprocal(rinv[:, :], sq[:, 1, :]))
                newton(rinv[:, :], sq[:, 0, :], acc[:, :])
                then(dve.tensor_tensor(rinv[:, :], rinv[:, :], acc[:, :], ALU.mult))

            def ffn_up(base, F):
                with dve.Fori(0, FT // 2) as i:
                    for k in range(2):
                        f = 2 * i + k
                        g, t, v = F["gate"][:, k, :], F["tanh"][:, k, :], F["up"][:, k, :]
                        dve.wait_ge(unit_used, base + 2 * f + 1)
                        dve.tensor_tensor(g, psum[:, 4 + 2 * k, :], rinv[:, :], ALU.mult).then_inc(F["gate_scaled"], 1)
                        dve.wait_ge(unit_used, base + 2 * f + 2)
                        dve.tensor_tensor(v, psum[:, 5 + 2 * k, :], rinv[:, :], ALU.mult).then_inc(F["up_scaled"], 1)
                        dve.wait_ge(F["gate_tanh"], f + 1)
                        dve.scalar_tensor_tensor(out=g, in0=t, scalar=1.0, in1=g, op0=ALU.add, op1=ALU.mult
                                                 ).then_inc(F["gate_silu"], 1)
                        dve.wait_ge(F["gate_silu"], f + 1)
                        dve.wait_ge(F["up_scaled"], f + 1)
                        dve.tensor_tensor(v, v, g, ALU.mult).then_inc(F["hidden"], 1)
                        dve.wait_ge(F["hidden_high"], f + 1)
                        dve.tensor_tensor(tile(F["hid_l"], f), v, tile(F["hid_h"], f), ALU.subtract
                                          ).then_inc(F["hidden_low"], 1)

            def down_half(b, F, half, n):
                def res(j):
                    if j < HALF - 1:
                        dve.wait_ge(F["down_tile"], (HALF - 1) * half + j + 1)
                    else:
                        dve.wait_ge(unit_used, b + DOWN)
                    residual(n, HALF * half + j, HALF * half + j, 0.25, h_ready[n] if n else final_ready)

                def lowp(j):
                    scale_low(n, HALF * half + j)

                if not n:
                    for j in range(HALF):
                        res(j)
                    return
                res(0)
                res(1)
                lowp(0)
                res(2)
                lowp(1)
                res(3)
                lowp(2)
                lowp(3)
                for j in range(HALF):
                    c = HALF * half + j
                    add_square(n, c, c)

            clear_sum(0)
            dve.wait_ge(small_landed, 32)
            dve.tensor_scalar(half_bias[:, :], params[:, P_BIAS:P_BIAS + 2 * DT], 0.5, None, ALU.mult
                              ).then_inc(init_done, 1)
            for c in range(DT):
                scale_low(0, c)
            for c in range(DT):
                add_square(0, c, c)
            norm_factor(0)
            ffn_up(U_GU1, ffn1)
            clear_sum(1)
            down_half(U_DN1, ffn1, 0, 1)
            down_half(U_DN1 + DOWN, ffn1, 1, 1)

            norm_factor(1)
            dve.memset(xp[:, 0:PAD], 0.0)
            then(dve.memset(win[:, :, 0:PAD], 0.0))

            def scaled(u, to, done):
                dve.wait_ge(unit_used, u + 1)
                dve.tensor_tensor(to, psum[:, 4 + u % SLOTS, :], rinv[:, :], ALU.mult).then_inc(done, 1)

            def pooling(g):
                w = POOL_WINDOWS[g]
                if g:
                    dve.wait_ge(pooled_low, g)
                scaled(U_POOL + g, xp[:, PAD:PAD + TOK], pool_scaled)
                dve.wait_ge(pool_scaled, g + 1)
                src, k = xp[:, :], 1
                for n in range(g + 1):
                    to = win[:, n % 2, :]
                    then(dve.tensor_tensor(to[:, PAD:PAD + TOK], src[:, PAD:PAD + TOK],
                                           src[:, PAD - k:PAD - k + TOK], ALU.add))
                    src, k = to, 2 * k
                then(dve.scalar_tensor_tensor(out=pooled[:, :], in0=src[:, PAD:PAD + TOK], scalar=1.0 / w,
                                              in1=xp[:, PAD:PAD + TOK], op0=ALU.mult, op1=ALU.subtract))
                inv = consts[:, C_INV + g * PAD:C_INV + g * PAD + w]
                then(dve.tensor_tensor(src[:, PAD:PAD + w], src[:, PAD:PAD + w], inv, ALU.mult))
                dve.tensor_tensor(pooled[:, 0:w], src[:, PAD:PAD + w], xp[:, PAD:PAD + w], ALU.subtract
                                  ).then_inc(pooled_ready, 1)
                dve.wait_ge(pooled_high, g + 1)
                dve.tensor_tensor(pl_l[:, g, :], pooled[:, :], pl_h[:, g, :], ALU.subtract).then_inc(pooled_low, 1)

            def mixed_part(g):
                dve.wait_ge(mixed_high, g + 1)
                dve.scalar_tensor_tensor(out=mix_l[:, g, :], in0=psum[:, g % 2, :],
                                         scalar=params[:, P_PSC + g:P_PSC + g + 1], in1=mix_h[:, g, :],
                                         op0=ALU.mult, op1=ALU.subtract).then_inc(mixed_low, 1)

            pooling(0)
            dve.wait_ge(pw_high, 1)
            dve.tensor_tensor(pw_l[:, :], pw_raw[:, :], pw_h[:, :], ALU.subtract).then_inc(pw_low, 1)
            for g in range(1, PG):
                pooling(g)
            scaled(U_K, kraw[:, :], k_scaled)
            scaled(U_V, vraw[:, :], v_scaled)
            scaled(U_Q, q[:, 0, :], q_ready)
            dve.memset(kn[:, 0:BLK], 0.0).then_inc(k_ready, 1)
            dve.memset(vtok[:, 0, :], 0.0).then_inc(v_ready, 1)
            scaled(U_Q + 1, q[:, 1, :], q_ready)
            mixed_part(0)
            mixed_part(1)
            scaled(U_Q + 2, q[:, 2, :], q_ready)
            mixed_part(2)
            mixed_part(3)
            dve.wait_ge(k_summed, 1)
            dve.tensor_scalar(sq[:, 1, :], psum[:, 3, :], 1.0 / HD, EPS, ALU.mult, ALU.add).then_inc(k_var, 1)
            scaled(U_Q + 3, q[:, 3, :], q_ready)
            dve.wait_ge(k_root, 1)
            then(dve.reciprocal(acc[:, :], sq[:, 0, :]))
            newton(acc[:, :], sq[:, 1, :], sq[:, 0, :])
            then(dve.tensor_tensor(acc[:, :], acc[:, :], sq[:, 0, :], ALU.mult))
            dve.scalar_tensor_tensor(out=kn[:, BLK:BLK + TOK], in0=kraw[:, :], scalar=params[:, P_KN:P_KN + 1],
                                     in1=acc[:, :], op0=ALU.mult, op1=ALU.mult).then_inc(k_ready, 1)
            scaled(U_Q + 4, q[:, 4, :], q_ready)
            dve.wait_ge(v_turned, 1)
            dve.tensor_copy(vtok[:, 1:1 + NB, :].rearrange("p a b -> p (a b)"), psum[:, 3, :]).then_inc(v_ready, 1)
            for c in range(5, QT):
                scaled(U_Q + c, q[:, c, :], q_ready)
            dve.wait_ge(q_summed, QT)
            dve.tensor_scalar(qtmp[:, 0, :], psum[:, 2, 0:NB * QT * KV], 1.0 / HD, EPS, ALU.mult, ALU.add
                              ).then_inc(q_var, 1)
            dve.wait_ge(q_root, 1)
            then(dve.reciprocal(rq[:, :], qtmp[:, 1, :]))
            newton(rq[:, :], qtmp[:, 0, :], qtmp[:, 2, :])
            then(dve.scalar_tensor_tensor(out=rq[:, :], in0=rq[:, :], scalar=float(HD) ** -0.5, in1=qtmp[:, 2, :],
                                          op0=ALU.mult, op1=ALU.mult))

            def stage(nb):
                dve.wait_ge(q_block_high, nb + 1)
                dve.scalar_tensor_tensor(out=qs_l[:, :, :], in0=q[:, :, bass.ds(nb * BLK, BLK)],
                                         scalar=params[:, P_QN:P_QN + 1], in1=qs_h[:, :, :],
                                         op0=ALU.mult, op1=ALU.subtract).then_inc(q_block_low, 1)

            def block_factors(nb):
                if isinstance(nb, int) and nb == 0:
                    pass
                else:
                    dve.wait_ge(exp_done, 20 * nb)
                dve.tensor_copy(rqn[:, :], rq[:, bass.ds(nb * QT * KV, QT * KV)]).then_inc(rq_now_ready, 1)

            def maxima(nb, j):
                b = j % 2
                dve.wait_ge(mask_set, 1)
                dve.wait_ge(scored, 4 * nb + j + 1)
                dve.memset(spare[:, :], 0.0)
                for a in range(4):
                    hh, kv = a // KV, a % KV
                    dve.tensor_tensor_reduce(prob[:, b, a, :], psum[:, 4 + kv, hh * 2 * BLK:(hh + 1) * 2 * BLK],
                                             mask[:, :], 1.0, 4 * MASKED, ALU.add, ALU.max,
                                             smax[:, b, a:a + 1]).then_inc(masked, 1)
                dve.wait_ge(masked, 16 * nb + 4 * j + 5)
                dve.wait_ge(rq_now_ready, nb + 1)
                dve.tensor_tensor(smx[:, b, :], smax[:, b, :], rqn[:, 4 * j:4 * j + 4], ALU.mult).then_inc(max_a, 1)
                dve.wait_ge(max_a, 4 * nb + j + 1)
                sink = params[:, P_SINK + 4 * j:P_SINK + 4 * j + 4]
                dve.tensor_tensor(smx[:, b, :], smx[:, b, :], sink, ALU.max).then_inc(max_b, 1)
                dve.wait_ge(max_b, 4 * nb + j + 1)
                dve.tensor_scalar(nmax[:, b, :], smx[:, b, :], -1.0, None, ALU.mult).then_inc(max_done, 1)
                dve.tensor_tensor(msink[:, b, :], sink, smx[:, b, :], ALU.subtract).then_inc(max_done, 1)

            def denominators(nb, j):
                b = j % 2
                dve.wait_ge(exp_done, 20 * nb + 5 * j + 5)
                dve.tensor_tensor(den[:, b, :], rows[:, b, :], esink[:, b, :], ALU.add).then_inc(den_done, 1)
                dve.wait_ge(den_done, 4 * nb + j + 1)
                dve.reciprocal(rden[:, b, :], den[:, b, :]).then_inc(rden_done, 1)

            def gate(nb, j):
                dve.wait_ge(unit_used, U_GATE + SLOTS * nb + j + 1)
                dve.tensor_tensor(gt[:, j % 2, :], psum[:, (1, 2, 3, 2)[j], :], rinv[:, :], ALU.mult
                                  ).then_inc(gate_scaled, 1)

            def pool_gate(nb, j):
                dve.wait_ge(gate_tanh, 4 * nb + j + 1)
                m = tile(pb, 2 * nb + j)
                dve.scalar_tensor_tensor(out=m, in0=gt[:, j, :], scalar=1.0, in1=m, op0=ALU.add, op1=ALU.mult
                                         ).then_inc(pool_gated, 1)

            def turned_part(nb, j):
                for k in range(2):
                    dve.wait_ge(pt_high, 8 * nb + 2 * j + k + 1)
                    dve.tensor_tensor(pt_l[:, k, :], psum[:, 6 + k, :], pt_h[:, k, :], ALU.subtract).then_inc(pt_low, 1)

            def attn_part(nb, j):
                for kv in range(KV):
                    dve.wait_ge(attn_high, 8 * nb + 2 * j + kv + 1)
                    r = slice(kv * HD, (kv + 1) * HD)
                    at_block = (r, slice(2 * j, 2 * j + 2), bass.ds(nb * BLK, BLK))
                    dve.tensor_tensor(ol[at_block],
                                      psum[r, 0, kv * 2 * BLK:(kv + 1) * 2 * BLK].rearrange("p (a t) -> p a t", a=2),
                                      oh[at_block], ALU.subtract).then_inc(attn_low, 1)

            def attention_block(nb, last):
                maxima(nb, 0)
                gate(nb, 0)
                denominators(nb, 0)
                maxima(nb, 1)
                pool_gate(nb, 0)
                gate(nb, 1)
                denominators(nb, 1)
                turned_part(nb, 0)
                maxima(nb, 2)
                pool_gate(nb, 1)
                attn_part(nb, 0)
                gate(nb, 2)
                denominators(nb, 2)
                turned_part(nb, 1)
                maxima(nb, 3)
                attn_part(nb, 1)
                denominators(nb, 3)
                turned_part(nb, 2)
                gate(nb, 3)
                if not last:
                    dve.tensor_copy(mask[:, :], consts[:, C_MASK:C_MASK + 2 * BLK]).then_inc(mask_set, 1)
                    block_factors(nb + 1)
                    stage(nb + 1)
                attn_part(nb, 2)
                turned_part(nb, 3)
                attn_part(nb, 3)

            dve.memset(mask[:, 0:BLK], MASKED).then_inc(mask_set, 1)
            dve.tensor_copy(mask[:, BLK:2 * BLK], consts[:, C_MASK + BLK:C_MASK + 2 * BLK]).then_inc(masked, 1)
            block_factors(0)
            dve.memset(den[:, :, :], 0.0).then_inc(attn_low, 1)
            stage(0)
            with dve.Fori(0, NB - 1) as nb:
                attention_block(nb, False)
            attention_block(NB - 1, True)

            with dve.Fori(0, 2) as i:
                for j in range(SLOTS):
                    m = SLOTS * i + j
                    o = gt[:, j % 2, :]
                    dve.wait_ge(unit_used, U_AO + m + 1)
                    dve.scalar_tensor_tensor(out=o, in0=tile(th_attn, m), scalar=1.0, in1=psum[:, 4 + j, :],
                                             op0=ALU.add, op1=ALU.mult).then_inc(attn_gated, 1)
                    dve.wait_ge(attn_gated, m + 1)
                    dve.tensor_tensor(o, o, tile(pb, m), ALU.add).then_inc(merged, 1)
                    dve.wait_ge(merged_high, m + 1)
                    dve.tensor_tensor(tile(mg_l, m), o, tile(mg_h, m), ALU.subtract).then_inc(merged_low, 1)

            clear_sum(2)
            for c in range(DT):
                dve.wait_ge(unit_used, U_WO + c + 1)
                residual(2, c, c % SLOTS, 0.5, h_ready[2])
                scale_low(2, c)
                add_square(2, c, c)
            norm_factor(2)
            ffn_up(U_GU2, ffn2)
            down_half(U_DN2, ffn2, 0, 0)
            down_half(U_DN2 + DOWN, ffn2, 1, 0)


def _tiles(w):
    return w.reshape(w.shape[0] // P, P, w.shape[1] // P, P).transpose(0, 2, 1, 3)


def _unit(tiles):
    return np.concatenate(list(tiles), axis=1)


def _weight_stream(w):
    def ffn(gate, up, down):
        g, u, d = _tiles(gate), _tiles(up), _tiles(down)
        for f in range(FT):
            yield _unit(g[:, f])
            yield _unit(u[:, f])
        for half in range(2):
            for c2 in range(DOWN):
                yield _unit(d[2 * c2 + kk, HALF * half + m] for m in range(HALF) for kk in range(2))

    def pair(a):
        return a.reshape(a.shape[0], KV, QT, HD).transpose(0, 2, 1, 3).reshape(a.shape[0], -1)

    yield from ffn(w["ffn1_w_gate"], w["ffn1_w_up"], w["ffn1_w_down"])
    w_in = w["w_in"]
    edges = np.cumsum([0, PG * P, QT * P, P, P, D, D])
    wp, wq, wk, wv, wgp, wga = [w_in[:, a:b] for a, b in zip(edges[:-1], edges[1:])]
    for part in (wp, wk, wv, pair(wq)):
        t = _tiles(part)
        for n in range(t.shape[1]):
            yield _unit(t[:, n])
    t = _tiles(w["w_pool_out"])
    for i in range(PG):
        yield _unit(t[c, 2 * i + m] for m in range(2) for c in range(PG))
    tp, ta = _tiles(wgp), _tiles(wga)
    for nb in range(NB):
        for t in (tp, ta):
            for k in range(2):
                yield _unit(t[:, 2 * nb + k])
    for m in (np.ascontiguousarray(pair(w["w_attn_out"].T).T), w["w_out"]):
        t = _tiles(m)
        for n in range(DT):
            yield _unit(t[:, n])
    yield from ffn(w["ffn2_w_gate"], w["ffn2_w_up"], w["ffn2_w_down"])


def _constants():
    c = np.zeros((P, CONSTS), np.float32)
    i = np.arange(P)
    c[:, C_ONES:C_ONES + P] = 1.0
    c[:, C_ID:C_ID + P] = np.eye(P)
    c[:, C_HEADS:C_HEADS + P] = (i[:, None] // HD) == (i[None] // HD)
    before = np.where(i[None] > i[:, None], 0.0, MASKED)
    own = np.where(i[None] <= i[:, None], 0.0, MASKED)
    c[:, C_MASK:C_MASK + 2 * P] = np.concatenate([before, own], 1)
    for g, w in enumerate(POOL_WINDOWS):
        c[:, C_INV + g * PAD:C_INV + (g + 1) * PAD] = 1.0 / np.minimum(np.arange(PAD) + 1, w)
    return c


def kernel(**inputs):
    import concourse.bacc as _bacc
    from concourse.bass_utils import run_bass_kernel_spmd as _run

    w = {k: np.asarray(v) for k, v in inputs.items()}

    def cols(v):
        return v.reshape(-1, P).T

    bias = w["gate_bias"].reshape(2, NB, 2, P).transpose(1, 0, 2, 3)
    sinks = w["sinks"].reshape(KV, QT).T.reshape(1, -1)
    params = np.concatenate([
        cols(w["ffn1_norm"]), cols(w["mix_norm"]), cols(w["ffn2_norm"]), cols(w["pool_scale"]),
        np.tile(w["q_norm"], KV)[:, None], np.tile(w["k_norm"], KV)[:, None],
        bias.reshape(-1, P).T, np.repeat(sinks, P, axis=0)], axis=1)
    arrays = {
        "x": np.ascontiguousarray(w["x"][0].T.reshape(DT, P, TOK).transpose(1, 0, 2)),
        "consts": _constants(),
        "params": np.ascontiguousarray(params),
        "poolw": np.ascontiguousarray(w["pool_w"].transpose(1, 0, 2).reshape(P, PG * P)),
        "weights": np.stack(list(_weight_stream(w))),
    }
    nc = _bacc.Bacc("TRN2", target_bir_lowering=False, num_devices=1)
    args = [nc.dram_tensor(f"{n}_dram", a.shape, F32, kind="ExternalInput").ap() for n, a in arrays.items()]
    args.append(nc.dram_tensor("out_dram", (P, DT, TOK), F32, kind="ExternalOutput").ap())
    layer_kernel(nc, *args)
    r = _run(nc, [{f"{n}_dram": a for n, a in arrays.items()}], core_ids=[0])
    got = r.results[0]["out_dram"]
    return np.ascontiguousarray(got.transpose(1, 0, 2).reshape(D, TOK).T)[None]
```

```python
from contextlib import ExitStack

import numpy as np

import concourse.bass as bass
from concourse import mybir

F32 = mybir.dt.float32
F32R = mybir.dt.float32r
ALU = mybir.AluOpType
ACT = mybir.ActivationFunctionType

P = 128
TOK = 512
D = 1024
DT = D // P
FF = 2816
FT = FF // P
POOL_WINDOWS = (2, 4, 8, 16)
PG = len(POOL_WINDOWS)
PAD = max(POOL_WINDOWS)
HD = 64
KV = 2
QT = 8
BLK = 128
NB = TOK // BLK
EPS = 1e-6
MASKED = -1e30

SLOTS = 4
TILES = 8
UNIT = TILES * P
HALF = DT // 2
DOWN = FT * HALF // TILES

U_GU1 = 0
U_DN1 = U_GU1 + 2 * FT
U_POOL = U_DN1 + 2 * DOWN
U_K = U_POOL + PG
U_V = U_K + 1
U_Q = U_V + 1
U_PO = U_Q + QT
U_GATE = U_PO + PG
U_AO = U_GATE + 2 * DT
U_WO = U_AO + DT
U_GU2 = U_WO + DT
U_DN2 = U_GU2 + 2 * FT
UNITS = U_DN2 + 2 * DOWN

X_PIECES = (0, 1, 2, 4, 6, DT)

C_ONES, C_ID, C_HEADS, C_MASK, C_INV = 0, 128, 256, 384, 640
CONSTS = C_INV + PG * PAD
P_N1, P_MIX, P_N2, P_PSC, P_QN, P_KN, P_BIAS, P_SINK = 0, 8, 16, 24, 28, 29, 30, 46
PARAMS = 62


def layer_kernel(nc, x_in, consts_in, params_in, poolw_in, weights_in, out):
    ctx = ExitStack()
    with ctx:
        def sb(name, shape, dt=F32, at=ctx):
            return at.enter_context(nc.sbuf_tensor(name, shape, dt))

        def sem(name):
            return ctx.enter_context(nc.semaphore(name))

        h = sb("h", [P, DT, TOK])
        raw = sb("w_raw", [P, SLOTS, UNIT])
        high = sb("w_high", [P, SLOTS, UNIT], F32R)
        low = sb("w_low", [P, SLOTS, UNIT], F32R)
        consts = sb("consts", [P, CONSTS])
        params = sb("params", [P, PARAMS])
        half_bias = sb("half_bias", [P, 2 * DT])
        rinv = sb("rinv", [P, TOK])
        sq = sb("squares", [P, 2, TOK])
        gt = sq
        acc = sb("sum_of_squares", [P, TOK])
        ones = consts[:, C_ONES:C_ONES + P]
        ident = consts[:, C_ID:C_ID + P]
        same_head = consts[:, C_HEADS:C_HEADS + P]
        head_cols = consts[:, C_HEADS:C_HEADS + P:HD]

        with ExitStack() as u_scope:
            uh = sb("u_high", [P, DT, TOK], F32R, u_scope)
            ul = sb("u_low", [P, DT, TOK], F32R, u_scope)
            with ExitStack() as s:
                ffn1 = dict(
                    hid_h=sb("hid1_high", [P, FT, TOK], F32R, s), hid_l=sb("hid1_low", [P, FT, TOK], F32R, s),
                    gate=sb("gate1", [P, 2, TOK], F32, s), tanh=sb("tanh1", [P, 2, TOK], F32, s),
                    up=sb("up1", [P, 2, TOK], F32, s))
            with ExitStack() as s:
                pb = sb("pool_branch", [P, DT, TOK], F32, s)
                with ExitStack() as t:
                    kraw = sb("k_raw", [P, TOK], F32, t)
                    vraw = sb("v_raw", [P, TOK], F32, t)
                    qsq = sb("q_squares", [P, 2, TOK], F32, t)
                    pw_raw = sb("poolw_raw", [P, PG * P], F32, t)
                    pw_h = sb("poolw_high", [P, PG * P], F32R, t)
                    pw_l = sb("poolw_low", [P, PG * P], F32R, t)
                th_attn = sb("tanh_gate_attn", [P, DT, TOK], F32, s)
                kn = sb("k_normed", [P, BLK + TOK], F32, s)
                vtok = sb("v_tokens", [P, 1 + NB, P], F32, s)
                rq = sb("rq", [P, NB * QT * KV], F32, s)
                qtmp = sb("rq_tmp", [P, 3, NB * QT * KV], F32, s)
                with ExitStack() as t:
                    q = sb("q", [P, QT, TOK], F32, t)
                with ExitStack() as t:
                    oh = sb("attn_high", [P, QT, TOK], F32R, t)
                    with ExitStack() as v:
                        pl_h = sb("pooled_high", [P, PG, TOK], F32R, v)
                        pl_l = sb("pooled_low", [P, PG, TOK], F32R, v)
                    ol = sb("attn_low", [P, QT, TOK], F32R, t)
                    with ExitStack() as v:
                        mix_h = sb("mixed_high", [P, PG, TOK], F32R, v)
                        mix_l = sb("mixed_low", [P, PG, TOK], F32R, v)
                        xp = sb("pool_in", [P, PAD + TOK], F32, v)
                        win = sb("window_sums", [P, 2, PAD + TOK], F32, v)
                        pooled = sb("pooled", [P, TOK], F32, v)
                    with ExitStack() as v:
                        prob = sb("probs", [P, 2, 4, 2 * BLK], F32, v)
                        pt_h = sb("probsT_high", [P, 2, 4 * BLK], F32R, v)
                        pt_l = sb("probsT_low", [P, 2, 4 * BLK], F32R, v)
                        qs_h = sb("q_block_high", [P, QT, BLK], F32R, v)
                        qs_l = sb("q_block_low", [P, QT, BLK], F32R, v)
                        ks_h = sb("k_block_high", [P, 2 * BLK], F32R, v)
                        ks_l = sb("k_block_low", [P, 2 * BLK], F32R, v)
                        vs_h = sb("v_block_high", [P, 2, P], F32R, v)
                        vs_l = sb("v_block_low", [P, 2, P], F32R, v)
                        mask = sb("mask_now", [P, 2 * BLK], F32, v)
                        smax = sb("raw_max", [P, 2, 4], F32, v)
                        msink = sb("sink_minus_max", [P, 2, 4], F32, v)
                        smx = sb("score_max", [P, 2, 4], F32, v)
                        nmax = sb("neg_max", [P, 2, 4], F32, v)
                        rows = sb("row_sums", [P, 2, 4], F32, v)
                        esink = sb("exp_sink", [P, 2, 4], F32, v)
                        den = sb("denominator", [P, 2, 4], F32, v)
                        rden = sb("inv_denominator", [P, 2, 4], F32, v)
                        spare = sb("spare", [P, 1], F32, v)
                        rqn = sb("rq_now", [P, QT * KV], F32, v)
        with ExitStack() as s:
            mg_h = sb("merged_high", [P, DT, TOK], F32R, s)
            mg_l = sb("merged_low", [P, DT, TOK], F32R, s)
        with ExitStack() as s:
            ffn2 = dict(
                hid_h=sb("hid2_high", [P, FT, TOK], F32R, s), hid_l=sb("hid2_low", [P, FT, TOK], F32R, s),
                gate=sb("gate2", [P, 2, TOK], F32, s), tanh=sb("tanh2", [P, 2, TOK], F32, s),
                up=sb("up2", [P, 2, TOK], F32, s))
            uh2 = sb("u2_high", [P, DT, TOK], F32R, s)
            ul2 = sb("u2_low", [P, DT, TOK], F32R, s)
        psum = ctx.enter_context(nc.psum_tensor("psum", [P, 8, TOK], F32))

        raw_landed = [sem(f"raw_landed{s}") for s in range(SLOTS)]
        first_landed = sem("first_landed")
        first_high = sem("first_high")
        first_low = sem("first_low")
        high_done = sem("high_done")
        low_done = sem("low_done")
        unit_used = sem("unit_used")
        params_landed = sem("params_landed")
        consts_landed = sem("consts_landed")
        poolw_landed = sem("poolw_landed")
        x_landed = [sem(f"x_landed{i}") for i in range(len(X_PIECES) - 1)]
        init_done = sem("init_done")
        pw_high = sem("pw_high")
        pw_low = sem("pw_low")
        h_ready = [None] + [sem(f"h_ready{n}") for n in (1, 2)]
        u_high = [sem(f"u_high_done{n}") for n in range(3)]
        u_low = [sem(f"u_low_done{n}") for n in range(3)]
        squared = [sem(f"squared{n}") for n in range(3)]
        summed = [sem(f"summed{n}") for n in range(3)]
        ss_ready = sem("ss_ready")
        var_ready = sem("var_ready")
        root_ready = sem("root_ready")
        link = sem("vector_link")
        for n, f in enumerate((ffn1, ffn2)):
            for name in ("gate_scaled", "gate_tanh", "gate_silu", "up_scaled", "hidden", "hidden_high",
                         "hidden_low", "down_tile"):
                f[name] = sem(f"ffn{n + 1}_{name}")
        pool_scaled = sem("pool_scaled")
        pooled_ready = sem("pooled_ready")
        pooled_high = sem("pooled_high_done")
        pooled_low = sem("pooled_low_done")
        mixed_done = sem("mixed_done")
        mixed_high = sem("mixed_high_done")
        mixed_low = sem("mixed_low_done")
        k_scaled = sem("k_scaled")
        k_squared = sem("k_squared")
        k_summed = sem("k_summed")
        k_var = sem("k_var")
        k_root = sem("k_root")
        k_ready = sem("k_ready")
        v_scaled = sem("v_scaled")
        v_turned = sem("v_turned")
        v_ready = sem("v_ready")
        q_ready = sem("q_ready")
        q_squared = sem("q_squared")
        q_summed = sem("q_summed")
        q_var = sem("q_var")
        q_root = sem("q_root")
        rq_ready = sem("rq_ready")
        pb_ready = sem("pb_ready")
        q_block_high = sem("q_block_high_done")
        q_block_low = sem("q_block_low_done")
        k_block_high = sem("k_block_high_done")
        k_block_low = sem("k_block_low_done")
        v_block_high = sem("v_block_high_done")
        v_block_low = sem("v_block_low_done")
        rq_now_ready = sem("rq_now_ready")
        scored = sem("scored")
        mask_set = sem("mask_set")
        masked = sem("masked")
        max_a = sem("max_scaled")
        max_b = sem("max_with_sink")
        max_done = sem("max_done")
        exp_done = sem("exp_done")
        den_done = sem("den_done")
        rden_done = sem("rden_done")
        probs_ready = sem("probs_ready")
        turned = sem("probs_turned")
        pt_high = sem("pt_high_done")
        pt_low = sem("pt_low_done")
        weighed = sem("weighed")
        attn_high = sem("attn_high_done")
        attn_low = sem("attn_low_done")
        gate_scaled = sem("gate_scaled")
        gate_tanh = sem("gate_tanh")
        pool_gated = sem("pool_gated")
        attn_gated = sem("attn_gated")
        merged = sem("merged")
        merged_high = sem("merged_high_done")
        merged_low = sem("merged_low_done")
        final_ready = sem("final_ready")
        stored = sem("stored")

        gains = (params[:, P_N1:P_N1 + DT], params[:, P_MIX:P_MIX + DT], params[:, P_N2:P_N2 + DT])
        u_of = ((uh, ul), (uh, ul), (uh2, ul2))

        def lows(u):
            return u - 1

        def at(t, k, n=1):
            return t[:, bass.ds(k, n)]

        block = ctx.enter_context(nc.Block())

        @block.sync
        def _(sp):
            def load(u, s):
                sp.dma_start(raw[:, s, :], weights_in[bass.ds(u, 1), :, :].rearrange("a p n -> p (a n)")
                             ).then_inc(raw_landed[s], 16)

            def load_x(i):
                c = slice(X_PIECES[i], X_PIECES[i + 1])
                sp.dma_start(h[:, c, :], x_in[:, c, :]).then_inc(x_landed[i], 16)

            sp.dma_start(params[:, :], params_in).then_inc(params_landed, 16)
            load_x(0)
            sp.dma_start(raw[:, 0, 0:UNIT // 2], weights_in[0, :, 0:UNIT // 2]).then_inc(first_landed, 16)
            load_x(1)
            sp.dma_start(raw[:, 0, UNIT // 2:UNIT], weights_in[0, :, UNIT // 2:UNIT]).then_inc(raw_landed[0], 16)
            for i in range(2, len(X_PIECES) - 1):
                load_x(i)
            load(1, 1)
            load(2, 2)
            sp.dma_start(consts[:, :], consts_in).then_inc(consts_landed, 16)
            load(3, 3)
            sp.wait_ge(first_low, 4)
            load(4, 0)
            load(5, 1)
            for u in (6, 7):
                sp.wait_ge(low_done, lows(u - SLOTS))
                load(u, u % SLOTS)
            with sp.Fori(2, UNITS // SLOTS) as i:
                for s in range(SLOTS):
                    sp.wait_ge(low_done, lows(SLOTS * i + s - SLOTS))
                    load(SLOTS * i + s, s)
            for u in range(UNITS // SLOTS * SLOTS, UNITS):
                sp.wait_ge(low_done, lows(u - SLOTS))
                load(u, u % SLOTS)
            for c in range(DT):
                sp.wait_ge(final_ready, c + 1)
                sp.dma_start(out[:, c, :], h[:, c, :]).then_inc(stored, 16)
            sp.wait_ge(stored, 16 * DT)

        @block.tensor
        def _(pe):
            def passes(bank, s, tile, xh, xl, start, stop):
                wh = high[:, s, tile * P:(tile + 1) * P]
                wl = low[:, s, tile * P:(tile + 1) * P]
                o = psum[:, bank, :]
                pe.matmul(o, wh, xh, start=start, stop=False)
                pe.matmul(o, wh, xl, start=False, stop=False)
                return pe.matmul(o, wl, xh, start=False, stop=stop)

            def project(u, s, bank, xh, xl, x_ready=None, tiles=range(TILES), first_lows=None):
                if tiles[0] == 0 and first_lows is None:
                    pe.wait_ge(low_done, lows(u))
                for c in tiles:
                    if first_lows is not None and c % HALF == 0:
                        pe.wait_ge(first_low, first_lows[c // HALF])
                    if x_ready is not None:
                        pe.wait_ge(x_ready, c + 1)
                    mm = passes(bank, s, c, xh[:, c, :], xl[:, c, :], c == 0, c == TILES - 1)
                if tiles[-1] == TILES - 1:
                    mm.then_inc(unit_used, 1)

            def sum_of_squares(n):
                if n == 0:
                    pe.wait_ge(consts_landed, 16)
                pe.wait_ge(summed[n], DT + 1)
                pe.matmul(psum[:, 0, :], ones, acc[:, :], start=True, stop=True).then_inc(ss_ready, 1)

            def gate_up(base, f, k, F, xh, xl):
                pe.wait_ge(F["gate_scaled"], f - 1)
                project(base + 2 * f, 2 * k, 4 + 2 * k, xh, xl)
                pe.wait_ge(F["up_scaled"], f - 1)
                project(base + 2 * f + 1, 2 * k + 1, 5 + 2 * k, xh, xl)

            def ffn_up(n, base, F, xh, xl):
                project(base, 0, 4, xh, xl, u_low[n], first_lows=None if n else (1, 2))
                if n:
                    sum_of_squares(n)
                project(base + 1, 1, 5, xh, xl, first_lows=None if n else (3, 4))
                project(base + 2, 2, 6, xh, xl, tiles=range(0, TILES // 2))
                if not n:
                    sum_of_squares(n)
                project(base + 2, 2, 6, xh, xl, tiles=range(TILES // 2, TILES))
                project(base + 3, 3, 7, xh, xl)
                with pe.Fori(1, FT // 2) as i:
                    for k in range(2):
                        gate_up(base, 2 * i + k, k, F, xh, xl)

            def down_unit(u, s, c2, half, F, start=False, stop=False):
                pe.wait_ge(low_done, lows(u))
                for m in range(HALF):
                    for kk in range(2):
                        xh = F["hid_h"][:, bass.ds(2 * c2 + kk, 1), :].rearrange("p a t -> p (a t)")
                        xl = F["hid_l"][:, bass.ds(2 * c2 + kk, 1), :].rearrange("p a t -> p (a t)")
                        mm = passes(HALF * half + m, s, 2 * m + kk, xh, xl,
                                    start and kk == 0, stop and kk == 1)
                    if stop and m < HALF - 1:
                        mm.then_inc(F["down_tile"], 1)
                mm.then_inc(unit_used, 1)

            def ffn_down(base, F):
                for half in range(2):
                    b = base + half * DOWN
                    pe.wait_ge(F["hidden_low"], FT if half else FT - 2)
                    down_unit(b, b % SLOTS, 0, half, F, start=True)
                    with pe.Fori(0, 2) as i:
                        for j in range(SLOTS):
                            down_unit(b + 1 + SLOTS * i + j, (b + 1 + j) % SLOTS, 1 + SLOTS * i + j, half, F)
                    down_unit(b + DOWN - 2, (b + DOWN - 2) % SLOTS, DOWN - 2, half, F)
                    pe.wait_ge(F["hidden_low"], FT)
                    down_unit(b + DOWN - 1, (b + DOWN - 1) % SLOTS, DOWN - 1, half, F, stop=True)

            ffn_up(0, U_GU1, ffn1, uh, ul)
            ffn_down(U_DN1, ffn1)

            def proj_bank(u):
                return 4 + (u - U_POOL) % SLOTS

            def proj(u, x_ready=None, tiles=range(TILES)):
                project(u, u % SLOTS, proj_bank(u), uh, ul, x_ready, tiles)

            def pool_mix(g):
                pe.wait_ge(pooled_low, g + 1)
                if g == 0:
                    pe.wait_ge(pw_low, 1)
                if g >= 2:
                    pe.wait_ge(mixed_low, g - 1)
                o, w = psum[:, g % 2, :], slice(g * P, (g + 1) * P)
                pe.matmul(o, pw_h[:, w], pl_h[:, g, :], start=True, stop=False)
                pe.matmul(o, pw_h[:, w], pl_l[:, g, :], start=False, stop=False)
                pe.matmul(o, pw_l[:, w], pl_h[:, g, :], start=False, stop=True).then_inc(mixed_done, 1)

            def q_sums(c):
                pe.wait_ge(q_squared, c + 1)
                for b in range(NB):
                    col = b * QT * KV + c * KV
                    mm = pe.matmul(psum[:, 2, col:col + KV], qsq[:, c % 2, b * BLK:(b + 1) * BLK], head_cols,
                                   start=True, stop=True, skip_group_check=True)
                mm.then_inc(q_summed, 1)

            pe.wait_ge(h_ready[1], HALF + 1)
            proj(U_POOL, u_low[1])
            pe.wait_ge(h_ready[1], DT)
            proj(U_POOL + 1, tiles=range(0, TILES // 2))
            sum_of_squares(1)
            proj(U_POOL + 1, tiles=range(TILES // 2, TILES))
            proj(U_POOL + 2)
            proj(U_POOL + 3)
            pe.wait_ge(pool_scaled, 1)
            proj(U_K)
            pe.wait_ge(pool_scaled, 2)
            proj(U_V)
            pe.wait_ge(pool_scaled, 3)
            proj(U_Q)
            pe.wait_ge(pool_scaled, 4)
            proj(U_Q + 1)
            q_sums(0)
            pool_mix(0)
            pool_mix(1)
            pe.wait_ge(k_scaled, 1)
            proj(U_Q + 2)
            q_sums(1)
            pool_mix(2)
            pool_mix(3)
            pe.wait_ge(k_squared, 1)
            pe.matmul(psum[:, 3, :], same_head, sq[:, 0, :], start=True, stop=True).then_inc(k_summed, 1)
            pe.wait_ge(v_scaled, 1)
            proj(U_Q + 3)
            q_sums(2)
            pe.wait_ge(k_var, 1)
            for b in range(NB):
                mm = pe.transpose(psum[:, 3, b * P:(b + 1) * P], vraw[:, b * BLK:(b + 1) * BLK], ident)
            mm.then_inc(v_turned, 1)
            for c in range(4, QT):
                pe.wait_ge(q_ready, c - 3)
                proj(U_Q + c)
                q_sums(c - 1)
            pe.wait_ge(mixed_low, PG)
            for i in range(PG):
                u = U_PO + i
                pe.wait_ge(low_done, lows(u))
                if i < 2:
                    pe.wait_ge(q_ready, 6 + 2 * i)
                else:
                    pe.wait_ge(pb_ready, 2 * i - 2)
                for m in range(2):
                    for c in range(PG):
                        mm = passes(6 - 2 * (i % 2) + m, u % SLOTS, m * PG + c, mix_h[:, c, :], mix_l[:, c, :],
                                    c == 0, c == PG - 1)
                mm.then_inc(unit_used, 1)
                if i == 0:
                    q_sums(QT - 1)

            def scores(nb, j):
                pe.wait_ge(masked, 16 * nb + 4 * j + 1)
                if j == 0:
                    pe.wait_ge(q_block_low, nb + 1)
                    pe.wait_ge(k_block_low, nb + 1)
                for hh in range(2):
                    for n, (qs, ks) in enumerate(((qs_h, ks_h), (qs_h, ks_l), (qs_l, ks_h))):
                        for kv in range(KV):
                            r = slice(kv * HD, (kv + 1) * HD)
                            mm = pe.matmul(psum[:, 4 + kv, hh * 2 * BLK:(hh + 1) * 2 * BLK],
                                           qs[r, 2 * j + hh, :], ks[r, :], start=(n == 0), stop=(n == 2))
                mm.then_inc(scored, 1)

            def gate(nb, j, tiles=range(TILES)):
                project(U_GATE + SLOTS * nb + j, j, (1, 2, 3, 2)[j], uh, ul, tiles=tiles)

            def turn(nb, j):
                pe.wait_ge(probs_ready, 4 * nb + j + 1)
                for k in range(2):
                    for a in range(4):
                        hh, kv = a // KV, a % KV
                        col = (kv * 2 + hh) * BLK
                        mm = pe.transpose(psum[:, 6 + k, col:col + BLK], prob[:, j % 2, a, k * BLK:(k + 1) * BLK], ident)
                mm.then_inc(turned, 1)

            def weigh(nb, j):
                pe.wait_ge(pt_low, 8 * nb + 2 * j + 2)
                pe.wait_ge(attn_low, 8 * nb + 2 * j + 1)
                if j == 0:
                    pe.wait_ge(v_block_low, nb + 1)
                o = psum[:, 0, :]
                for k in range(2):
                    pe.matmul(o, vs_h[:, k, :], pt_h[:, k, :], start=(k == 0), stop=False)
                    pe.matmul(o, vs_h[:, k, :], pt_l[:, k, :], start=False, stop=False)
                    mm = pe.matmul(o, vs_l[:, k, :], pt_h[:, k, :], start=False, stop=(k == 1))
                mm.then_inc(weighed, 1)

            def step(nb, j):
                before = (nb, j - 1) if j else (nb - 1, SLOTS - 1)
                scores(nb, j)
                gate(nb, j, range(0, TILES // 2))
                turn(*before)
                gate(nb, j, range(TILES // 2, TILES))
                weigh(*before)

            gate(0, 0, range(0, 2))
            pe.wait_ge(pb_ready, DT)
            scores(0, 0)
            gate(0, 0, range(2, TILES))
            with pe.Fori(0, NB - 1) as nb:
                for j in range(1, SLOTS):
                    step(nb, j)
                step(nb + 1, 0)
            for j in range(1, SLOTS):
                step(NB - 1, j)

            early, late = range(0, TILES // 2), range(TILES // 2, TILES)
            pe.wait_ge(masked, 16 * NB + 1)
            pe.wait_ge(attn_low, 8 * NB - 3)
            project(U_AO, 0, 4, oh, ol, tiles=early)
            turn(NB - 1, SLOTS - 1)
            project(U_AO + 1, 1, 5, oh, ol, tiles=early)
            weigh(NB - 1, SLOTS - 1)
            project(U_AO, 0, 4, oh, ol, tiles=range(TILES // 2, TILES - 2))
            pe.wait_ge(attn_low, 8 * NB + 1)
            project(U_AO, 0, 4, oh, ol, tiles=range(TILES - 2, TILES))
            project(U_AO + 1, 1, 5, oh, ol, tiles=late)
            project(U_AO + 2, 2, 6, oh, ol)
            project(U_AO + 3, 3, 7, oh, ol)
            for j in range(SLOTS):
                pe.wait_ge(attn_gated, j + 1)
                project(U_AO + SLOTS + j, j, 4 + j, oh, ol)

            for j in range(SLOTS):
                project(U_WO + j, j, j, mg_h, mg_l, merged_low if j == 0 else None)
            for j in range(SLOTS):
                pe.wait_ge(h_ready[2], j + 1)
                project(U_WO + SLOTS + j, j, j, mg_h, mg_l)

            ffn_up(2, U_GU2, ffn2, uh2, ul2)
            ffn_down(U_DN2, ffn2)

        @block.scalar
        def _(act):
            def refill(u, s, i=0, first=False):
                if not first:
                    act.wait_ge(unit_used, u - SLOTS + 1)
                act.wait_ge(raw_landed[s], 16 * i)
                act.activation(high[:, s, :], raw[:, s, :], ACT.Copy).then_inc(high_done, 1)

            def next_unit(u0, i=0):
                refill(u0 + SLOTS + SLOTS * i, u0 % SLOTS, u0 // SLOTS + 2 + i)

            def scale_high(n, c):
                if n:
                    act.wait_ge(h_ready[n], c + 1)
                else:
                    act.wait_ge(x_landed[sum(c >= first for first in X_PIECES[1:])], 16)
                act.activation(u_of[n][0][:, bass.ds(c, 1), :], h[:, bass.ds(c, 1), :], ACT.Identity,
                               scale=at(gains[n], c)).then_inc(u_high[n], 1)

            def square(n, c, k):
                act.wait_ge(summed[n], c - 2 + 2 if k >= 2 else 1)
                act.activation(sq[:, k % 2, :], h[:, bass.ds(c, 1), :].rearrange("p a t -> p (a t)"),
                               ACT.Square).then_inc(squared[n], 1)

            def root(n):
                act.wait_ge(var_ready, n + 1)
                act.activation(sq[:, 1, :], sq[:, 0, :], ACT.Sqrt).then_inc(root_ready, 1)

            def ffn_up(base, F):
                with act.Fori(0, FT // 2) as i:
                    for k in range(2):
                        f = 2 * i + k
                        next_unit(base + 2 * k, i)
                        act.wait_ge(F["gate_scaled"], f + 1)
                        act.activation(F["tanh"][:, k, :], F["gate"][:, k, :], ACT.Tanh, scale=0.5
                                       ).then_inc(F["gate_tanh"], 1)
                        next_unit(base + 2 * k + 1, i)
                        act.wait_ge(F["hidden"], f + 1)
                        act.activation(F["hid_h"][:, bass.ds(f, 1), :], F["up"][:, k:k + 1, :], ACT.Copy
                                       ).then_inc(F["hidden_high"], 1)

            def down_half(b, n, half):
                with act.Fori(0, 2) as i:
                    for j in range(SLOTS):
                        next_unit(b + j, i)
                for u in (b + 8, b + 9):
                    if u + SLOTS < UNITS:
                        next_unit(u)
                if n:
                    for j in range(HALF):
                        scale_high(n, HALF * half + j)
                if b + 10 + SLOTS < UNITS:
                    next_unit(b + 10)
                if n:
                    for j in range(HALF):
                        c = HALF * half + j
                        square(n, c, c)

            act.wait_ge(params_landed, 16)
            act.activation(half_bias[:, :], params[:, P_BIAS:P_BIAS + 2 * DT], ACT.Copy, scale=0.5).then_inc(init_done, 1)
            scale_high(0, 0)
            act.wait_ge(first_landed, 16)
            act.activation(high[:, 0, 0:UNIT // 2], raw[:, 0, 0:UNIT // 2], ACT.Copy).then_inc(first_high, 1)
            scale_high(0, 1)
            act.wait_ge(raw_landed[0], 16)
            act.activation(high[:, 0, UNIT // 2:UNIT], raw[:, 0, UNIT // 2:UNIT], ACT.Copy).then_inc(high_done, 1)
            for c in range(2, DT):
                scale_high(0, c)
            act.wait_ge(raw_landed[1], 16)
            act.activation(high[:, 1, 0:UNIT // 2], raw[:, 1, 0:UNIT // 2], ACT.Copy).then_inc(first_high, 1)
            act.activation(high[:, 1, UNIT // 2:UNIT], raw[:, 1, UNIT // 2:UNIT], ACT.Copy).then_inc(high_done, 1)
            for c in range(DT):
                square(0, c, c)
                if c == 3:
                    refill(2, 2, 1, first=True)
            refill(3, 3, 1, first=True)
            root(0)
            ffn_up(U_GU1, ffn1)
            down_half(U_DN1, 1, 0)
            down_half(U_DN1 + DOWN, 1, 1)

            def stage_qk(nb):
                if not (isinstance(nb, int) and nb == 0):
                    act.wait_ge(scored, 4 * nb)
                act.activation(qs_h[:, :, :], q[:, :, bass.ds(nb * BLK, BLK)], ACT.Identity,
                               scale=params[:, P_QN:P_QN + 1]).then_inc(q_block_high, 1)
                act.activation(ks_h[:, :], kn[:, bass.ds(nb * BLK, 2 * BLK)], ACT.Copy).then_inc(k_block_high, 1)

            def stage_v(nb):
                if not (isinstance(nb, int) and nb == 0):
                    act.wait_ge(weighed, 4 * nb)
                act.activation(vs_h[:, :, :], vtok[:, bass.ds(nb, 2), :], ACT.Copy).then_inc(v_block_high, 1)

            def pooled_part(g):
                act.wait_ge(pooled_ready, g + 1)
                act.activation(pl_h[:, g, :], pooled[:, :], ACT.Copy).then_inc(pooled_high, 1)

            def mixed_part(g):
                act.wait_ge(mixed_done, g + 1)
                act.activation(mix_h[:, g, :], psum[:, g % 2, :], ACT.Identity,
                               scale=params[:, P_PSC + g:P_PSC + g + 1]).then_inc(mixed_high, 1)

            def q_square(c):
                act.wait_ge(q_ready, c + 1)
                if c >= 2:
                    act.wait_ge(q_summed, c - 1)
                act.activation(qsq[:, c % 2, :], q[:, c, :], ACT.Square).then_inc(q_squared, 1)

            act.wait_ge(h_ready[1], DT)
            act.dma_start(pw_raw[:, :], poolw_in).then_inc(poolw_landed, 16)
            root(1)
            next_unit(U_POOL)
            act.wait_ge(poolw_landed, 16)
            act.activation(pw_h[:, :], pw_raw[:, :], ACT.Copy).then_inc(pw_high, 1)
            pooled_part(0)
            next_unit(U_POOL + 1)
            pooled_part(1)
            next_unit(U_POOL + 2)
            pooled_part(2)
            next_unit(U_POOL + 3)
            next_unit(U_K)
            pooled_part(3)
            next_unit(U_V)
            act.wait_ge(k_scaled, 1)
            act.activation(sq[:, 0, :], kraw[:, :], ACT.Square).then_inc(k_squared, 1)
            q_square(0)
            next_unit(U_Q)
            mixed_part(0)
            mixed_part(1)
            q_square(1)
            next_unit(U_Q + 1)
            mixed_part(2)
            mixed_part(3)
            q_square(2)
            next_unit(U_Q + 2)
            act.wait_ge(k_var, 1)
            act.activation(sq[:, 0, :], sq[:, 1, :], ACT.Sqrt).then_inc(k_root, 1)
            for c in range(3, QT):
                q_square(c)
                next_unit(U_Q + c)
            act.wait_ge(k_ready, 2)
            act.wait_ge(v_ready, 2)
            stage_qk(0)
            stage_v(0)
            for i in range(PG):
                for m in range(2):
                    act.wait_ge(unit_used, U_PO + i + 1)
                    act.activation(pb[:, 2 * i + m, :], psum[:, 6 - 2 * (i % 2) + m, :], ACT.Copy
                                   ).then_inc(pb_ready, 1)
                next_unit(U_PO + i)
                if i == 1:
                    act.wait_ge(q_var, 1)
                    act.activation(qtmp[:, 1, :], qtmp[:, 0, :], ACT.Sqrt).then_inc(q_root, 1)

            def exps(nb, j):
                act.wait_ge(max_done, 8 * nb + 2 * j + 2)
                for a in range(4):
                    act.activation(prob[:, j % 2, a, :], prob[:, j % 2, a, :], ACT.Exp,
                                   bias=nmax[:, j % 2, a:a + 1], scale=rqn[:, 4 * j + a:4 * j + a + 1],
                                   accum_out=rows[:, j % 2, a:a + 1]).then_inc(exp_done, 1)
                act.activation(esink[:, j % 2, :], msink[:, j % 2, :], ACT.Exp).then_inc(exp_done, 1)

            def gate(nb, j):
                act.wait_ge(init_done, 1)
                act.wait_ge(gate_scaled, 4 * nb + j + 1)
                to = gt[:, j:j + 1, :] if j < 2 else th_attn[:, bass.ds(2 * nb + j - 2, 1), :]
                act.activation(to, gt[:, j % 2:j % 2 + 1, :], ACT.Tanh, scale=0.5,
                               bias=half_bias[:, bass.ds(4 * nb + j, 1)]).then_inc(gate_tanh, 1)

            def turned_part(nb, j):
                act.wait_ge(turned, 4 * nb + j + 1)
                for k in range(2):
                    act.activation(pt_h[:, k, :], psum[:, 6 + k, :], ACT.Copy).then_inc(pt_high, 1)

            def attn_part(nb, j):
                act.wait_ge(weighed, 4 * nb + j + 1)
                for kv in range(KV):
                    r = slice(kv * HD, (kv + 1) * HD)
                    act.activation(oh[r, 2 * j:2 * j + 2, bass.ds(nb * BLK, BLK)],
                                   psum[r, 0, kv * 2 * BLK:(kv + 1) * 2 * BLK].rearrange("p (a t) -> p a t", a=2),
                                   ACT.Copy).then_inc(attn_high, 1)

            def step(nb, j):
                before = (nb, j - 1) if j else (nb - 1, SLOTS - 1)
                if j == SLOTS - 1 and not (isinstance(nb, int) and nb == NB - 1):
                    stage_qk(nb + 1)
                turned_part(*before)
                exps(nb, j)
                next_unit(U_GATE + j, nb)
                gate(nb, j)
                attn_part(*before)
                if j == 0:
                    stage_v(nb)

            exps(0, 0)
            next_unit(U_GATE)
            gate(0, 0)
            with act.Fori(0, NB - 1) as nb:
                for j in range(1, SLOTS):
                    step(nb, j)
                step(nb + 1, 0)
            for j in range(1, SLOTS):
                step(NB - 1, j)
            turned_part(NB - 1, SLOTS - 1)
            attn_part(NB - 1, SLOTS - 1)

            def merge_part(i, j):
                m = SLOTS * i + j
                next_unit(U_AO + j, i)
                act.wait_ge(merged, m + 1)
                act.activation(mg_h[:, bass.ds(m, 1), :], gt[:, j % 2:j % 2 + 1, :], ACT.Copy).then_inc(merged_high, 1)

            with act.Fori(0, 2) as i:
                for j in range(SLOTS):
                    merge_part(i, j)

            for half in range(2):
                for j in range(SLOTS):
                    c = HALF * half + j
                    next_unit(U_WO + c)
                    scale_high(2, c)
                    square(2, c, c)
            root(2)
            ffn_up(U_GU2, ffn2)
            down_half(U_DN2, 0, 0)
            b = U_DN2 + DOWN
            with act.Fori(0, 1) as i:
                for j in range(SLOTS):
                    next_unit(b + j, i)
            for u in range(b + SLOTS, UNITS - SLOTS):
                next_unit(u)

        @block.gpsimd
        def _(pool):
            def low_part(u, s):
                pool.wait_ge(high_done, u + 1)
                pool.tensor_tensor(low[:, s, :], raw[:, s, :], high[:, s, :], ALU.subtract).then_inc(low_done, 1)

            low_part(2, 2)
            low_part(3, 3)
            with pool.Fori(1, U_GATE // SLOTS) as i:
                for s in range(SLOTS):
                    low_part(SLOTS * i + s, s)

            def stage_k(nb):
                pool.wait_ge(k_block_high, nb + 1)
                pool.tensor_tensor(ks_l[:, :], kn[:, bass.ds(nb * BLK, 2 * BLK)], ks_h[:, :],
                                   ALU.subtract).then_inc(k_block_low, 1)

            def stage_v(nb):
                pool.wait_ge(v_block_high, nb + 1)
                pool.tensor_tensor(vs_l[:, :, :], vtok[:, bass.ds(nb, 2), :], vs_h[:, :, :],
                                   ALU.subtract).then_inc(v_block_low, 1)

            def normalize(nb, j):
                pool.wait_ge(rden_done, 4 * nb + j + 1)
                p = prob[:, j % 2, :, :]
                pool.tensor_tensor(p, p, rden[:, j % 2, :].unsqueeze(2).to_broadcast([P, 4, 2 * BLK]),
                                   ALU.mult).then_inc(probs_ready, 1)

            def step(nb, j):
                if j == SLOTS - 1 and not (isinstance(nb, int) and nb == NB - 1):
                    stage_k(nb + 1)
                normalize(nb, j)
                low_part(U_GATE + SLOTS + SLOTS * nb + j, j)
                if j == 0 and not (isinstance(nb, int) and nb == 0):
                    stage_v(nb)

            stage_k(0)
            stage_v(0)
            for s in range(SLOTS):
                low_part(U_GATE + s, s)
            step(0, 0)
            with pool.Fori(0, NB - 1) as nb:
                for j in range(1, SLOTS):
                    step(nb, j)
                step(nb + 1, 0)
            for j in range(1, SLOTS):
                step(NB - 1, j)
            with pool.Fori(U_AO // SLOTS + 1, UNITS // SLOTS) as i:
                for s in range(SLOTS):
                    low_part(SLOTS * i + s, s)
            for u in range(UNITS // SLOTS * SLOTS, UNITS):
                low_part(u, u % SLOTS)

        @block.vector
        def _(dve):
            steps = [0]

            def then(ins):
                steps[0] += 1
                ins.then_inc(link, 1)
                dve.wait_ge(link, steps[0])

            def tile(t, c):
                return t[:, bass.ds(c, 1), :].rearrange("p a t -> p (a t)")

            def clear_sum(n):
                dve.memset(acc[:, :], 0.0).then_inc(summed[n], 1)

            def scale_low(n, c):
                dve.wait_ge(u_high[n], c + 1)
                hi, lo = u_of[n]
                dve.scalar_tensor_tensor(out=tile(lo, c), in0=tile(h, c), scalar=at(gains[n], c), in1=tile(hi, c),
                                         op0=ALU.mult, op1=ALU.subtract).then_inc(u_low[n], 1)

            def add_square(n, c, k):
                dve.wait_ge(squared[n], c + 1)
                dve.wait_ge(summed[n], c + 1)
                dve.tensor_tensor(acc[:, :], acc[:, :], sq[:, k % 2, :], ALU.add).then_inc(summed[n], 1)

            def residual(n, c, bank, scale, done):
                dve.scalar_tensor_tensor(out=tile(h, c), in0=psum[:, bank, :], scalar=scale, in1=tile(h, c),
                                         op0=ALU.mult, op1=ALU.add).then_inc(done, 1)

            def newton(y, v, t):
                then(dve.tensor_tensor(t, y, y, ALU.mult))
                then(dve.tensor_tensor(t, t, v, ALU.mult))
                then(dve.tensor_scalar(t, t, -0.5, 1.5, ALU.mult, ALU.add))

            def norm_factor(n):
                dve.wait_ge(ss_ready, n + 1)
                dve.tensor_scalar(sq[:, 0, :], psum[:, 0, :], 1.0 / D, EPS, ALU.mult, ALU.add).then_inc(var_ready, 1)
                dve.wait_ge(root_ready, n + 1)
                then(dve.reciprocal(rinv[:, :], sq[:, 1, :]))
                newton(rinv[:, :], sq[:, 0, :], acc[:, :])
                then(dve.tensor_tensor(rinv[:, :], rinv[:, :], acc[:, :], ALU.mult))

            def ffn_up(base, F):
                with dve.Fori(0, FT // 2) as i:
                    for k in range(2):
                        f = 2 * i + k
                        g, t, v = F["gate"][:, k, :], F["tanh"][:, k, :], F["up"][:, k, :]
                        dve.wait_ge(unit_used, base + 2 * f + 1)
                        dve.tensor_tensor(g, psum[:, 4 + 2 * k, :], rinv[:, :], ALU.mult).then_inc(F["gate_scaled"], 1)
                        dve.wait_ge(unit_used, base + 2 * f + 2)
                        dve.tensor_tensor(v, psum[:, 5 + 2 * k, :], rinv[:, :], ALU.mult).then_inc(F["up_scaled"], 1)
                        dve.wait_ge(F["gate_tanh"], f + 1)
                        dve.scalar_tensor_tensor(out=g, in0=t, scalar=1.0, in1=g, op0=ALU.add, op1=ALU.mult
                                                 ).then_inc(F["gate_silu"], 1)
                        dve.wait_ge(F["gate_silu"], f + 1)
                        dve.wait_ge(F["up_scaled"], f + 1)
                        dve.tensor_tensor(v, v, g, ALU.mult).then_inc(F["hidden"], 1)
                        dve.wait_ge(F["hidden_high"], f + 1)
                        dve.tensor_tensor(tile(F["hid_l"], f), v, tile(F["hid_h"], f), ALU.subtract
                                          ).then_inc(F["hidden_low"], 1)

            def down_half(b, F, half, n):
                def res(j):
                    if j < HALF - 1:
                        dve.wait_ge(F["down_tile"], (HALF - 1) * half + j + 1)
                    else:
                        dve.wait_ge(unit_used, b + DOWN)
                    residual(n, HALF * half + j, HALF * half + j, 0.25, h_ready[n] if n else final_ready)

                def lowp(j):
                    scale_low(n, HALF * half + j)

                if not n:
                    for j in range(HALF):
                        res(j)
                    return
                res(0)
                res(1)
                lowp(0)
                res(2)
                lowp(1)
                res(3)
                lowp(2)
                lowp(3)
                for j in range(HALF):
                    c = HALF * half + j
                    add_square(n, c, c)

            clear_sum(0)
            dve.wait_ge(params_landed, 16)

            def first_part(s, part, ready, count):
                dve.wait_ge(ready, count)
                dve.tensor_tensor(low[:, s, part], raw[:, s, part], high[:, s, part], ALU.subtract
                                  ).then_inc(first_low, 1)

            scale_low(0, 0)
            first_part(0, slice(0, UNIT // 2), first_high, 1)
            scale_low(0, 1)
            first_part(0, slice(UNIT // 2, UNIT), high_done, 1)
            for c in range(2, DT):
                scale_low(0, c)
            first_part(1, slice(0, UNIT // 2), first_high, 2)
            first_part(1, slice(UNIT // 2, UNIT), high_done, 2)
            for c in range(DT):
                add_square(0, c, c)
            norm_factor(0)
            ffn_up(U_GU1, ffn1)
            clear_sum(1)
            down_half(U_DN1, ffn1, 0, 1)
            down_half(U_DN1 + DOWN, ffn1, 1, 1)

            norm_factor(1)
            dve.memset(xp[:, 0:PAD], 0.0)
            then(dve.memset(win[:, :, 0:PAD], 0.0))

            def scaled(u, to, done):
                dve.wait_ge(unit_used, u + 1)
                dve.tensor_tensor(to, psum[:, 4 + (u - U_POOL) % SLOTS, :], rinv[:, :], ALU.mult).then_inc(done, 1)

            def pooling(g):
                w = POOL_WINDOWS[g]
                if g:
                    dve.wait_ge(pooled_low, g)
                scaled(U_POOL + g, xp[:, PAD:PAD + TOK], pool_scaled)
                dve.wait_ge(pool_scaled, g + 1)
                src, k = xp[:, :], 1
                for n in range(g + 1):
                    to = win[:, n % 2, :]
                    then(dve.tensor_tensor(to[:, PAD:PAD + TOK], src[:, PAD:PAD + TOK],
                                           src[:, PAD - k:PAD - k + TOK], ALU.add))
                    src, k = to, 2 * k
                then(dve.scalar_tensor_tensor(out=pooled[:, :], in0=src[:, PAD:PAD + TOK], scalar=1.0 / w,
                                              in1=xp[:, PAD:PAD + TOK], op0=ALU.mult, op1=ALU.subtract))
                inv = consts[:, C_INV + g * PAD:C_INV + g * PAD + w]
                then(dve.tensor_tensor(src[:, PAD:PAD + w], src[:, PAD:PAD + w], inv, ALU.mult))
                dve.tensor_tensor(pooled[:, 0:w], src[:, PAD:PAD + w], xp[:, PAD:PAD + w], ALU.subtract
                                  ).then_inc(pooled_ready, 1)
                dve.wait_ge(pooled_high, g + 1)
                dve.tensor_tensor(pl_l[:, g, :], pooled[:, :], pl_h[:, g, :], ALU.subtract).then_inc(pooled_low, 1)

            def mixed_part(g):
                dve.wait_ge(mixed_high, g + 1)
                dve.scalar_tensor_tensor(out=mix_l[:, g, :], in0=psum[:, g % 2, :],
                                         scalar=params[:, P_PSC + g:P_PSC + g + 1], in1=mix_h[:, g, :],
                                         op0=ALU.mult, op1=ALU.subtract).then_inc(mixed_low, 1)

            pooling(0)
            dve.wait_ge(pw_high, 1)
            dve.tensor_tensor(pw_l[:, :], pw_raw[:, :], pw_h[:, :], ALU.subtract).then_inc(pw_low, 1)
            for g in range(1, PG):
                pooling(g)
            scaled(U_K, kraw[:, :], k_scaled)
            scaled(U_V, vraw[:, :], v_scaled)
            scaled(U_Q, q[:, 0, :], q_ready)
            dve.memset(kn[:, 0:BLK], 0.0).then_inc(k_ready, 1)
            dve.memset(vtok[:, 0, :], 0.0).then_inc(v_ready, 1)
            scaled(U_Q + 1, q[:, 1, :], q_ready)
            mixed_part(0)
            mixed_part(1)
            scaled(U_Q + 2, q[:, 2, :], q_ready)
            mixed_part(2)
            mixed_part(3)
            dve.wait_ge(k_summed, 1)
            dve.tensor_scalar(sq[:, 1, :], psum[:, 3, :], 1.0 / HD, EPS, ALU.mult, ALU.add).then_inc(k_var, 1)
            scaled(U_Q + 3, q[:, 3, :], q_ready)
            dve.wait_ge(k_root, 1)
            then(dve.reciprocal(acc[:, :], sq[:, 0, :]))
            newton(acc[:, :], sq[:, 1, :], sq[:, 0, :])
            then(dve.tensor_tensor(acc[:, :], acc[:, :], sq[:, 0, :], ALU.mult))
            dve.scalar_tensor_tensor(out=kn[:, BLK:BLK + TOK], in0=kraw[:, :], scalar=params[:, P_KN:P_KN + 1],
                                     in1=acc[:, :], op0=ALU.mult, op1=ALU.mult).then_inc(k_ready, 1)
            scaled(U_Q + 4, q[:, 4, :], q_ready)
            dve.wait_ge(v_turned, 1)
            dve.tensor_copy(vtok[:, 1:1 + NB, :].rearrange("p a b -> p (a b)"), psum[:, 3, :]).then_inc(v_ready, 1)
            for c in range(5, QT):
                scaled(U_Q + c, q[:, c, :], q_ready)
            def stage(nb):
                dve.wait_ge(q_block_high, nb + 1)
                dve.scalar_tensor_tensor(out=qs_l[:, :, :], in0=q[:, :, bass.ds(nb * BLK, BLK)],
                                         scalar=params[:, P_QN:P_QN + 1], in1=qs_h[:, :, :],
                                         op0=ALU.mult, op1=ALU.subtract).then_inc(q_block_low, 1)

            def block_factors(nb):
                if isinstance(nb, int) and nb == 0:
                    pass
                else:
                    dve.wait_ge(exp_done, 20 * nb)
                dve.tensor_copy(rqn[:, :], rq[:, bass.ds(nb * QT * KV, QT * KV)]).then_inc(rq_now_ready, 1)

            def maxima(nb, j):
                b = j % 2
                dve.wait_ge(mask_set, nb + 1)
                dve.wait_ge(scored, 4 * nb + j + 1)
                dve.memset(spare[:, :], 0.0)
                for a in range(4):
                    hh, kv = a // KV, a % KV
                    dve.tensor_tensor_reduce(prob[:, b, a, :], psum[:, 4 + kv, hh * 2 * BLK:(hh + 1) * 2 * BLK],
                                             mask[:, :], 1.0, 4 * MASKED, ALU.add, ALU.max,
                                             smax[:, b, a:a + 1]).then_inc(masked, 1)
                dve.wait_ge(masked, 16 * nb + 4 * j + 5)
                dve.wait_ge(rq_now_ready, nb + 1)
                dve.tensor_tensor(smx[:, b, :], smax[:, b, :], rqn[:, 4 * j:4 * j + 4], ALU.mult).then_inc(max_a, 1)
                dve.wait_ge(max_a, 4 * nb + j + 1)
                sink = params[:, P_SINK + 4 * j:P_SINK + 4 * j + 4]
                dve.tensor_tensor(smx[:, b, :], smx[:, b, :], sink, ALU.max).then_inc(max_b, 1)
                dve.wait_ge(max_b, 4 * nb + j + 1)
                dve.tensor_scalar(nmax[:, b, :], smx[:, b, :], -1.0, None, ALU.mult).then_inc(max_done, 1)
                dve.tensor_tensor(msink[:, b, :], sink, smx[:, b, :], ALU.subtract).then_inc(max_done, 1)

            def denominators(nb, j):
                b = j % 2
                dve.wait_ge(exp_done, 20 * nb + 5 * j + 5)
                dve.tensor_tensor(den[:, b, :], rows[:, b, :], esink[:, b, :], ALU.add).then_inc(den_done, 1)
                dve.wait_ge(den_done, 4 * nb + j + 1)
                dve.reciprocal(rden[:, b, :], den[:, b, :]).then_inc(rden_done, 1)

            def gate(nb, j):
                dve.wait_ge(unit_used, U_GATE + SLOTS * nb + j + 1)
                dve.tensor_tensor(gt[:, j % 2, :], psum[:, (1, 2, 3, 2)[j], :], rinv[:, :], ALU.mult
                                  ).then_inc(gate_scaled, 1)

            def pool_gate(nb, j):
                dve.wait_ge(gate_tanh, 4 * nb + j + 1)
                m = tile(pb, 2 * nb + j)
                dve.scalar_tensor_tensor(out=m, in0=gt[:, j, :], scalar=1.0, in1=m, op0=ALU.add, op1=ALU.mult
                                         ).then_inc(pool_gated, 1)

            def turned_part(nb, j):
                for k in range(2):
                    dve.wait_ge(pt_high, 8 * nb + 2 * j + k + 1)
                    dve.tensor_tensor(pt_l[:, k, :], psum[:, 6 + k, :], pt_h[:, k, :], ALU.subtract).then_inc(pt_low, 1)

            def attn_part(nb, j):
                for kv in range(KV):
                    dve.wait_ge(attn_high, 8 * nb + 2 * j + kv + 1)
                    r = slice(kv * HD, (kv + 1) * HD)
                    at_block = (r, slice(2 * j, 2 * j + 2), bass.ds(nb * BLK, BLK))
                    dve.tensor_tensor(ol[at_block],
                                      psum[r, 0, kv * 2 * BLK:(kv + 1) * 2 * BLK].rearrange("p (a t) -> p a t", a=2),
                                      oh[at_block], ALU.subtract).then_inc(attn_low, 1)

            dve.memset(mask[:, 0:BLK], MASKED).then_inc(mask_set, 1)
            dve.wait_ge(consts_landed, 16)
            dve.tensor_copy(mask[:, BLK:2 * BLK], consts[:, C_MASK + BLK:C_MASK + 2 * BLK]).then_inc(masked, 1)
            dve.memset(den[:, :, :], 0.0).then_inc(attn_low, 1)
            stage(0)
            dve.wait_ge(q_summed, QT)
            dve.tensor_scalar(qtmp[:, 0, :], psum[:, 2, 0:NB * QT * KV], 1.0 / HD, EPS, ALU.mult, ALU.add
                              ).then_inc(q_var, 1)
            dve.wait_ge(q_root, 1)
            then(dve.reciprocal(rq[:, :], qtmp[:, 1, :]))
            newton(rq[:, :], qtmp[:, 0, :], qtmp[:, 2, :])
            then(dve.scalar_tensor_tensor(out=rq[:, :], in0=rq[:, :], scalar=float(HD) ** -0.5, in1=qtmp[:, 2, :],
                                          op0=ALU.mult, op1=ALU.mult))

            block_factors(0)
            maxima(0, 0)
            denominators(0, 0)
            gate(0, 0)

            def step(nb, j):
                before = (nb, j - 1) if j else (nb - 1, SLOTS - 1)
                if j == 0:
                    dve.tensor_copy(mask[:, :], consts[:, C_MASK:C_MASK + 2 * BLK]).then_inc(mask_set, 1)
                    block_factors(nb)
                maxima(nb, j)
                if j == SLOTS - 1 and not (isinstance(nb, int) and nb == NB - 1):
                    stage(nb + 1)
                if j in (1, 2):
                    pool_gate(nb, j - 1)
                turned_part(*before)
                denominators(nb, j)
                gate(nb, j)
                attn_part(*before)

            with dve.Fori(0, NB - 1) as nb:
                for j in range(1, SLOTS):
                    step(nb, j)
                step(nb + 1, 0)
            for j in range(1, SLOTS):
                step(NB - 1, j)
            turned_part(NB - 1, SLOTS - 1)
            attn_part(NB - 1, SLOTS - 1)

            with dve.Fori(0, 2) as i:
                for j in range(SLOTS):
                    m = SLOTS * i + j
                    o = gt[:, j % 2, :]
                    dve.wait_ge(unit_used, U_AO + m + 1)
                    dve.scalar_tensor_tensor(out=o, in0=tile(th_attn, m), scalar=1.0, in1=psum[:, 4 + j, :],
                                             op0=ALU.add, op1=ALU.mult).then_inc(attn_gated, 1)
                    dve.wait_ge(attn_gated, m + 1)
                    dve.tensor_tensor(o, o, tile(pb, m), ALU.add).then_inc(merged, 1)
                    dve.wait_ge(merged_high, m + 1)
                    dve.tensor_tensor(tile(mg_l, m), o, tile(mg_h, m), ALU.subtract).then_inc(merged_low, 1)

            clear_sum(2)
            for c in range(DT):
                dve.wait_ge(unit_used, U_WO + c + 1)
                residual(2, c, c % SLOTS, 0.5, h_ready[2])
                scale_low(2, c)
                add_square(2, c, c)
            norm_factor(2)
            ffn_up(U_GU2, ffn2)
            down_half(U_DN2, ffn2, 0, 0)
            down_half(U_DN2 + DOWN, ffn2, 1, 0)


def _tiles(w):
    return w.reshape(w.shape[0] // P, P, w.shape[1] // P, P).transpose(0, 2, 1, 3)


def _unit(tiles):
    return np.concatenate(list(tiles), axis=1)


def _weight_stream(w):
    def ffn(gate, up, down):
        g, u, d = _tiles(gate), _tiles(up), _tiles(down)
        for f in range(FT):
            yield _unit(g[:, f])
            yield _unit(u[:, f])
        for half in range(2):
            for c2 in range(DOWN):
                yield _unit(d[2 * c2 + kk, HALF * half + m] for m in range(HALF) for kk in range(2))

    def pair(a):
        return a.reshape(a.shape[0], KV, QT, HD).transpose(0, 2, 1, 3).reshape(a.shape[0], -1)

    yield from ffn(w["ffn1_w_gate"], w["ffn1_w_up"], w["ffn1_w_down"])
    w_in = w["w_in"]
    edges = np.cumsum([0, PG * P, QT * P, P, P, D, D])
    wp, wq, wk, wv, wgp, wga = [w_in[:, a:b] for a, b in zip(edges[:-1], edges[1:])]
    for part in (wp, wk, wv, pair(wq)):
        t = _tiles(part)
        for n in range(t.shape[1]):
            yield _unit(t[:, n])
    t = _tiles(w["w_pool_out"])
    for i in range(PG):
        yield _unit(t[c, 2 * i + m] for m in range(2) for c in range(PG))
    tp, ta = _tiles(wgp), _tiles(wga)
    for nb in range(NB):
        for t in (tp, ta):
            for k in range(2):
                yield _unit(t[:, 2 * nb + k])
    for m in (np.ascontiguousarray(pair(w["w_attn_out"].T).T), w["w_out"]):
        t = _tiles(m)
        for n in range(DT):
            yield _unit(t[:, n])
    yield from ffn(w["ffn2_w_gate"], w["ffn2_w_up"], w["ffn2_w_down"])


def _constants():
    c = np.zeros((P, CONSTS), np.float32)
    i = np.arange(P)
    c[:, C_ONES:C_ONES + P] = 1.0
    c[:, C_ID:C_ID + P] = np.eye(P)
    c[:, C_HEADS:C_HEADS + P] = (i[:, None] // HD) == (i[None] // HD)
    before = np.where(i[None] > i[:, None], 0.0, MASKED)
    own = np.where(i[None] <= i[:, None], 0.0, MASKED)
    c[:, C_MASK:C_MASK + 2 * P] = np.concatenate([before, own], 1)
    for g, w in enumerate(POOL_WINDOWS):
        c[:, C_INV + g * PAD:C_INV + (g + 1) * PAD] = 1.0 / np.minimum(np.arange(PAD) + 1, w)
    return c


def kernel(**inputs):
    import concourse.bacc as _bacc
    from concourse.bass_utils import run_bass_kernel_spmd as _run

    w = {k: np.asarray(v) for k, v in inputs.items()}

    def cols(v):
        return v.reshape(-1, P).T

    bias = w["gate_bias"].reshape(2, NB, 2, P).transpose(1, 0, 2, 3)
    sinks = w["sinks"].reshape(KV, QT).T.reshape(1, -1)
    params = np.concatenate([
        cols(w["ffn1_norm"]), cols(w["mix_norm"]), cols(w["ffn2_norm"]), cols(w["pool_scale"]),
        np.tile(w["q_norm"], KV)[:, None], np.tile(w["k_norm"], KV)[:, None],
        bias.reshape(-1, P).T, np.repeat(sinks, P, axis=0)], axis=1)
    arrays = {
        "x": np.ascontiguousarray(w["x"][0].T.reshape(DT, P, TOK).transpose(1, 0, 2)),
        "consts": _constants(),
        "params": np.ascontiguousarray(params),
        "poolw": np.ascontiguousarray(w["pool_w"].transpose(1, 0, 2).reshape(P, PG * P)),
        "weights": np.stack(list(_weight_stream(w))),
    }
    nc = _bacc.Bacc("TRN2", target_bir_lowering=False, num_devices=1)
    args = [nc.dram_tensor(f"{n}_dram", a.shape, F32, kind="ExternalInput").ap() for n, a in arrays.items()]
    args.append(nc.dram_tensor("out_dram", (P, DT, TOK), F32, kind="ExternalOutput").ap())
    layer_kernel(nc, *args)
    r = _run(nc, [{f"{n}_dram": a for n, a in arrays.items()}], core_ids=[0])
    got = r.results[0]["out_dram"]
    return np.ascontiguousarray(got.transpose(1, 0, 2).reshape(D, TOK).T)[None]
```
